# Optimizing a Trainium2 kernel written in Bass

```python
import math
import jax, jax.numpy as jnp
from jax import lax
import numpy as np

D_MODEL = 2048
BATCH = 1
SEQ = 256
DEPTH = 1
DEC_BATCH = 8
DEC_SEQ = 8
PAST_LEN = 2048
PAGE_SIZE = 128

DH = 128
H_A = 8
HKV_A = 2
H_IDX = 16
D_IDX = 64
TOPK_IDX = 256
H_B = 8
HKV_B = 2
MOBA_BLOCK = 256
MOBA_TOPK = 3
H_C = 8
DK_C = 128
DV_C = 256
N_BUCKETS = 32
MAX_DIST = 128
D_FF = 5504
CONV_W = 3
EPS = 1e-6
ROPE_BASE = 10000.0
Q_BLOCK_A = 128
Q_BLOCK_B = 16
RET_CHUNK = 128

SPLITS = (H_A * DH, HKV_A * DH, HKV_A * DH, H_IDX * D_IDX, D_IDX, H_IDX,
          H_B * DH, HKV_B * DH, HKV_B * DH,
          H_C * DK_C, H_C * DK_C, H_C * DV_C, H_C * DV_C,
          3 * D_MODEL)
N_IN = sum(SPLITS)

kernel_name = 'hybrid_dsa_moba_retention_convffn_step'

def rmsnorm(x, g):
    xf = x.astype(jnp.float32)
    y = xf * lax.rsqrt(jnp.mean(xf * xf, axis=-1, keepdims=True) + EPS)
    return (y * g.astype(jnp.float32)).astype(x.dtype)

def t5_bucket(rel):
    n = jnp.maximum(rel, 0)
    max_exact = N_BUCKETS // 2
    nf = jnp.maximum(n, 1).astype(jnp.float32)
    large = max_exact + (jnp.log(nf / max_exact) / math.log(MAX_DIST / max_exact)
                         * (N_BUCKETS - max_exact)).astype(jnp.int32)
    large = jnp.minimum(large, N_BUCKETS - 1)
    return jnp.where(n < max_exact, n, large)

def to_blocks(x, qb):
    b, t = x.shape[:2]
    return jnp.moveaxis(x.reshape(b, t // qb, qb, *x.shape[2:]), 1, 0)

def from_blocks(y):
    y = jnp.moveaxis(y, 0, 1)
    return y.reshape(y.shape[0], y.shape[1] * y.shape[2], *y.shape[3:])

def rotary(x, pos):
    d = x.shape[-1]
    inv = ROPE_BASE ** (-jnp.arange(0, d, 2, dtype=jnp.float32) / d)
    ang = pos.astype(jnp.float32)[:, None] * inv[None, :]
    cos = jnp.cos(ang)[None, :, None, :]
    sin = jnp.sin(ang)[None, :, None, :]
    xf = x.astype(jnp.float32)
    x1, x2 = xf[..., :d // 2], xf[..., d // 2:]
    return jnp.concatenate([x1 * cos - x2 * sin, x1 * sin + x2 * cos], axis=-1)

def dsa_attention(q, k, v, q_idx, k_idx, w_idx, q_pos, bias_tab):
    b, t = q.shape[:2]
    l = k.shape[1]
    n_sel = min(TOPK_IDX, l // 4)
    grp = H_A // HKV_A
    qb = math.gcd(t, Q_BLOCK_A)
    k_pos = jnp.arange(l, dtype=jnp.int32)
    kif = k_idx.astype(jnp.float32)

    def one_block(xs):
        qh, qi, wi, qp = xs
        s = jnp.einsum('bqhd,bsd->bqhs', qi.astype(jnp.float32), kif) * (D_IDX ** -0.5)
        score = jnp.einsum('bqh,bqhs->bqs', wi.astype(jnp.float32) * (H_IDX ** -0.5), jax.nn.relu(s))
        score = jnp.where(k_pos[None, None, :] <= qp[None, :, None], score, -jnp.inf)
        _, sel = lax.top_k(score, n_sel)
        valid = sel <= qp[None, :, None]
        ks = jax.vmap(lambda kk, ii: kk[ii])(k, sel).astype(jnp.float32)
        vs = jax.vmap(lambda vv, ii: vv[ii])(v, sel).astype(jnp.float32)
        qg = qh.astype(jnp.float32).reshape(b, qb, HKV_A, grp, DH)
        logits = jnp.einsum('bqgrd,bqngd->bqgrn', qg, ks).reshape(b, qb, H_A, n_sel) * (DH ** -0.5)
        bias = jnp.transpose(bias_tab[t5_bucket(qp[None, :, None] - sel)], (0, 1, 3, 2))
        logits = jnp.where(valid[:, :, None, :], logits + bias, -jnp.inf)
        p = jax.nn.softmax(logits, axis=-1).reshape(b, qb, HKV_A, grp, n_sel)
        o = jnp.einsum('bqgrn,bqngd->bqgrd', p, vs)
        return o.reshape(b, qb, H_A * DH).astype(q.dtype)

    out = lax.map(one_block, (to_blocks(q, qb), to_blocks(q_idx, qb), to_blocks(w_idx, qb),
                              q_pos.reshape(t // qb, qb)))
    return from_blocks(out)

def moba_attention(q, k, v, q_pos, bias_tab):
    b, t = q.shape[:2]
    l = k.shape[1]
    grp = H_B // HKV_B
    nb = -(-l // MOBA_BLOCK)
    pad = nb * MOBA_BLOCK - l

    def blockify(x):
        x = jnp.pad(x, ((0, 0), (0, pad), (0, 0), (0, 0)))
        return jnp.transpose(x.reshape(b, nb, MOBA_BLOCK, HKV_B, DH), (0, 1, 3, 2, 4))

    kb, vb = blockify(k), blockify(v)
    k_mean = jnp.mean(kb.astype(jnp.float32), axis=3)
    n_sel = min(MOBA_TOPK, (l - 1) // MOBA_BLOCK)
    qb = math.gcd(t, Q_BLOCK_B)
    offs = jnp.arange(MOBA_BLOCK, dtype=jnp.int32)
    b_idx = jnp.arange(b)[:, None, None, None]
    h_kv = (jnp.arange(H_B) // grp)[None, None, :, None]
    h_all = jnp.arange(H_B)[None, None, :, None, None]
    scale = DH ** -0.5

    def one_block(xs):
        qh, qp = xs
        qf = qh.astype(jnp.float32)
        qg = qf.reshape(b, qb, HKV_B, grp, DH)
        own = qp // MOBA_BLOCK
        ko = kb[:, own].astype(jnp.float32)
        vo = vb[:, own].astype(jnp.float32)
        rel_o = qp[:, None] - (own[:, None] * MOBA_BLOCK + offs[None, :])
        lo = jnp.einsum('bqgrd,bqgsd->bqgrs', qg, ko).reshape(b, qb, H_B, MOBA_BLOCK) * scale
        bias_o = jnp.transpose(bias_tab[t5_bucket(rel_o)], (0, 2, 1))
        lo = jnp.where((rel_o >= 0)[None, :, None, :], lo + bias_o[None], -jnp.inf)
        vo_h = jnp.repeat(vo, grp, axis=2)
        if n_sel == 0:
            p = jax.nn.softmax(lo, axis=-1)
            o = jnp.einsum('bqhs,bqhsd->bqhd', p, vo_h)
        else:
            gate = jnp.einsum('bqgrd,bngd->bqgrn', qg, k_mean).reshape(b, qb, H_B, nb)
            past = jnp.arange(nb)[None, :] < own[:, None]
            gate = jnp.where(past[None, :, None, :], gate, -jnp.inf)
            _, sel = lax.top_k(gate, n_sel)
            valid = sel < own[None, :, None, None]
            ks = kb[b_idx, sel, h_kv].astype(jnp.float32)
            vs = vb[b_idx, sel, h_kv].astype(jnp.float32)
            rel_s = qp[None, :, None, None, None] - (sel[..., None] * MOBA_BLOCK + offs)
            ls = jnp.einsum('bqhd,bqhnsd->bqhns', qf, ks) * scale + bias_tab[t5_bucket(rel_s), h_all]
            ls = jnp.where(valid[..., None], ls, -jnp.inf).reshape(b, qb, H_B, n_sel * MOBA_BLOCK)
            logits = jnp.concatenate([ls, lo], axis=-1)
            vals = jnp.concatenate([vs.reshape(b, qb, H_B, n_sel * MOBA_BLOCK, DH), vo_h], axis=3)
            p = jax.nn.softmax(logits, axis=-1)
            o = jnp.einsum('bqhs,bqhsd->bqhd', p, vals)
        return o.reshape(b, qb, H_B * DH).astype(q.dtype)

    out = lax.map(one_block, (to_blocks(q, qb), q_pos.reshape(t // qb, qb)))
    return from_blocks(out)

def retention(q, k, v, s0):
    t = q.shape[1]
    c = math.gcd(t, RET_CHUNK)
    log_g = jnp.log1p(-jnp.exp2(-5.0 - jnp.arange(H_C, dtype=jnp.float32)))
    i = jnp.arange(c, dtype=jnp.float32)
    diff = i[:, None] - i[None, :]
    intra = jnp.where(diff[None] >= 0, jnp.exp(jnp.maximum(diff, 0.0)[None] * log_g[:, None, None]), 0.0)
    cross = jnp.exp((i[:, None] + 1.0) * log_g[None, :])
    tail = jnp.exp((c - 1.0 - i)[:, None] * log_g[None, :])
    chunk_decay = jnp.exp(c * log_g)

    def step(s, xs):
        qc, kc, vc = xs
        att = jnp.einsum('bihd,bjhd->bhij', qc, kc) * intra[None]
        o = (jnp.einsum('bhij,bjhv->bihv', att, vc)
             + jnp.einsum('bihd,bhdv->bihv', qc, s) * cross[None, :, :, None])
        s = s * chunk_decay[None, :, None, None] + jnp.einsum('bjhd,bjhv->bhdv', kc * tail[None, :, :, None], vc)
        return s, o

    s_fin, o = lax.scan(step, s0.astype(jnp.float32),
                        (to_blocks(q.astype(jnp.float32), c), to_blocks(k.astype(jnp.float32), c),
                         to_blocks(v.astype(jnp.float32), c)))
    return from_blocks(o), s_fin

def conv_ffn(h, conv_prev, ffn_up, ffn_gate, conv_w, conv_b, ffn_down):
    t = h.shape[1]
    u = h @ ffn_up
    g = h @ ffn_gate
    ext = jnp.concatenate([conv_prev.astype(u.dtype), u], axis=1)
    c = conv_b
    for j in range(CONV_W):
        c = c + conv_w[j] * ext[:, j:j + t]
    y = (jax.nn.gelu(c, approximate=False) * g) @ ffn_down
    return y, ext[:, t:]

def gather_pages(cache_l, page_table):
    pages = cache_l[page_table]
    return pages.reshape(pages.shape[0], pages.shape[1] * pages.shape[2], *pages.shape[3:])

def trunk_layer(x, q_pos, past, s0, cprev, rel_bias, norm_mix, w_in, ret_gn, w_pa, w_pb, w_pc, w_out,
                norm_ffn, ffn_up, ffn_gate, conv_w, conv_b, ffn_down):
    b, t = x.shape[:2]
    h = rmsnorm(x, norm_mix)
    z = h @ w_in
    cuts = np.cumsum(SPLITS)[:-1].tolist()
    qa, ka, va, qi, ki, wi, qb_, kb_, vb_, qc, kc, vc, gc, gates = jnp.split(z, cuts, axis=-1)
    qa = qa.reshape(b, t, H_A, DH)
    ka = ka.reshape(b, t, HKV_A, DH)
    va = va.reshape(b, t, HKV_A, DH)
    qi = qi.reshape(b, t, H_IDX, D_IDX)
    qb_ = qb_.reshape(b, t, H_B, DH)
    kb_ = kb_.reshape(b, t, HKV_B, DH)
    vb_ = vb_.reshape(b, t, HKV_B, DH)
    qc = qc.reshape(b, t, H_C, DK_C)
    kc = kc.reshape(b, t, H_C, DK_C)
    vc = vc.reshape(b, t, H_C, DV_C)
    if past is None:
        ka_all, va_all, ki_all, kb_all, vb_all = ka, va, ki, kb_, vb_
    else:
        pa_k, pa_v, pa_i, pb_k, pb_v = past
        ka_all = jnp.concatenate([pa_k.astype(ka.dtype), ka], axis=1)
        va_all = jnp.concatenate([pa_v.astype(va.dtype), va], axis=1)
        ki_all = jnp.concatenate([pa_i.astype(ki.dtype), ki], axis=1)
        kb_all = jnp.concatenate([pb_k.astype(kb_.dtype), kb_], axis=1)
        vb_all = jnp.concatenate([pb_v.astype(vb_.dtype), vb_], axis=1)
    o_a = dsa_attention(qa, ka_all, va_all, qi, ki_all, wi, q_pos, rel_bias[:, :H_A])
    o_b = moba_attention(qb_, kb_all, vb_all, q_pos, rel_bias[:, H_A:])
    o_c, s_new = retention(rotary(qc, q_pos), rotary(kc, q_pos) * (DK_C ** -0.5), vc, s0)
    o_c = o_c * lax.rsqrt(jnp.mean(o_c * o_c, axis=-1, keepdims=True) + EPS)
    o_c = (o_c.reshape(b, t, H_C * DV_C) * ret_gn.astype(jnp.float32)
           * jax.nn.silu(gc.astype(jnp.float32))).astype(x.dtype)
    g_a, g_b, g_c = jnp.split(gates, 3, axis=-1)
    m = (jax.nn.sigmoid(g_a) * (o_a @ w_pa) + jax.nn.sigmoid(g_b) * (o_b @ w_pb)
         + jax.nn.sigmoid(g_c) * (o_c @ w_pc))
    x = x + m @ w_out
    f, c_new = conv_ffn(rmsnorm(x, norm_ffn), cprev, ffn_up, ffn_gate, conv_w, conv_b, ffn_down)
    x = x + f
    return x, (ka, va, ki, kb_, vb_, s_new.astype(s0.dtype), c_new)

def setup_inputs(seed: int = 0) -> dict:
    key = jax.random.key(seed)
    ks = jax.random.split(key, 32)
    n_pages = PAST_LEN // PAGE_SIZE
    n_used = DEC_BATCH * n_pages
    n_pool = n_used + n_used // 4

    def nrm(k, shape, scale):
        return scale * jax.random.normal(k, shape, jnp.float32)

    return {
        'x_prompt': nrm(ks[0], (BATCH, SEQ, D_MODEL), 1.0),
        'x_sample': nrm(ks[1], (DEC_BATCH, DEC_SEQ, D_MODEL), 1.0),
        'cache_a_k': nrm(ks[2], (DEPTH, n_pool, PAGE_SIZE, HKV_A, DH), 1.0),
        'cache_a_v': nrm(ks[3], (DEPTH, n_pool, PAGE_SIZE, HKV_A, DH), 1.0),
        'cache_a_kidx': nrm(ks[4], (DEPTH, n_pool, PAGE_SIZE, D_IDX), 1.0),
        'cache_b_k': nrm(ks[5], (DEPTH, n_pool, PAGE_SIZE, HKV_B, DH), 1.0),
        'cache_b_v': nrm(ks[6], (DEPTH, n_pool, PAGE_SIZE, HKV_B, DH), 1.0),
        'state_ret': nrm(ks[7], (DEPTH, DEC_BATCH, H_C, DK_C, DV_C), 0.1),
        'state_conv': nrm(ks[8], (DEPTH, DEC_BATCH, CONV_W - 1, D_FF), 1.0),
        'page_table': jax.random.permutation(ks[9], n_pool)[:n_used].reshape(DEC_BATCH, n_pages).astype(jnp.int32),
        'rel_bias': nrm(ks[10], (N_BUCKETS, H_A + H_B), 0.1),
        'norm_mix': 1.0 + nrm(ks[11], (DEPTH, D_MODEL), 0.02),
        'w_in': nrm(ks[12], (DEPTH, D_MODEL, N_IN), D_MODEL ** -0.5),
        'ret_gn': 1.0 + nrm(ks[13], (DEPTH, H_C * DV_C), 0.02),
        'w_pa': nrm(ks[14], (DEPTH, H_A * DH, D_MODEL), (H_A * DH) ** -0.5),
        'w_pb': nrm(ks[15], (DEPTH, H_B * DH, D_MODEL), (H_B * DH) ** -0.5),
        'w_pc': nrm(ks[16], (DEPTH, H_C * DV_C, D_MODEL), (H_C * DV_C) ** -0.5),
        'w_out': nrm(ks[17], (DEPTH, D_MODEL, D_MODEL), D_MODEL ** -0.5),
        'norm_ffn': 1.0 + nrm(ks[18], (DEPTH, D_MODEL), 0.02),
        'ffn_up': nrm(ks[19], (DEPTH, D_MODEL, D_FF), D_MODEL ** -0.5),
        'ffn_gate': nrm(ks[20], (DEPTH, D_MODEL, D_FF), D_MODEL ** -0.5),
        'conv_w': nrm(ks[21], (DEPTH, CONV_W, D_FF), CONV_W ** -0.5),
        'conv_b': nrm(ks[22], (DEPTH, D_FF), 0.02),
        'ffn_down': nrm(ks[23], (DEPTH, D_FF, D_MODEL), D_FF ** -0.5),
        'norm_final': 1.0 + nrm(ks[24], (D_MODEL,), 0.02),
    }

def reference(x_prompt, x_sample, cache_a_k, cache_a_v, cache_a_kidx, cache_b_k, cache_b_v, state_ret, state_conv,
              page_table, rel_bias, norm_mix, w_in, ret_gn, w_pa, w_pb, w_pc, w_out, norm_ffn, ffn_up, ffn_gate,
              conv_w, conv_b, ffn_down, norm_final):
    bp, tp = x_prompt.shape[:2]
    ts = x_sample.shape[1]
    past_len = page_table.shape[1] * cache_a_k.shape[2]
    pos_p = jnp.arange(tp, dtype=jnp.int32)
    pos_s = past_len + jnp.arange(ts, dtype=jnp.int32)
    xp, xs = x_prompt, x_sample
    st_p, st_s = [], []
    for l in range(DEPTH):
        w_l = (rel_bias, norm_mix[l], w_in[l], ret_gn[l], w_pa[l], w_pb[l], w_pc[l], w_out[l], norm_ffn[l],
               ffn_up[l], ffn_gate[l], conv_w[l], conv_b[l], ffn_down[l])
        s0_p = jnp.zeros((bp, H_C, DK_C, DV_C), x_prompt.dtype)
        c0_p = jnp.zeros((bp, CONV_W - 1, D_FF), x_prompt.dtype)
        xp, sp = trunk_layer(xp, pos_p, None, s0_p, c0_p, *w_l)
        past = (gather_pages(cache_a_k[l], page_table), gather_pages(cache_a_v[l], page_table),
                gather_pages(cache_a_kidx[l], page_table), gather_pages(cache_b_k[l], page_table),
                gather_pages(cache_b_v[l], page_table))
        xs, ss = trunk_layer(xs, pos_s, past, state_ret[l], state_conv[l], *w_l)
        st_p.append(sp)
        st_s.append(ss)
    a_k_p, a_v_p, a_kidx_p, b_k_p, b_v_p, ret_p, conv_p = [jnp.stack(z) for z in zip(*st_p)]
    a_k_s, a_v_s, a_kidx_s, b_k_s, b_v_s, ret_s, conv_s = [jnp.stack(z) for z in zip(*st_s)]
    y_prompt = rmsnorm(xp, norm_final)
    y_sample = rmsnorm(xs, norm_final)
    return (y_prompt, y_sample, a_k_p, a_v_p, a_kidx_p, b_k_p, b_v_p, ret_p, conv_p,
            a_k_s, a_v_s, a_kidx_s, b_k_s, b_v_s, ret_s, conv_s)


_drawn_inputs = setup_inputs


def setup_inputs(seed=0):
    import zlib

    import numpy as np

    out = dict(_drawn_inputs(seed))
    spreads = {}
    factors = {'rel_bias': 3.631,
     'ret_gn': 7.763,
     'norm_ffn': 2.829,
     'conv_b': 5.413,
     'norm_final': 22.822,
     'cache_b_k': 3.86,
     'cache_b_v': 3.569,
     'cache_a_k': 2.745}
    for name, (base, spread) in spreads.items():
        noise = np.random.default_rng([zlib.crc32(name.encode()), seed]).standard_normal(out[name].shape)
        drawn = base * np.exp(spread * noise) if base else spread * noise
        out[name] = __import__('jax').numpy.asarray(drawn.astype(out[name].dtype))
    for name, factor in factors.items():
        out[name] = (out[name] * factor).astype(out[name].dtype)
    return out
```

```python
from contextlib import ExitStack, contextmanager

import numpy as np

import concourse.bass as bass
from concourse import mybir

ALU = mybir.AluOpType
ACT = mybir.ActivationFunctionType
F32 = mybir.dt.float32
F32R = mybir.dt.float32r
BF16 = mybir.dt.bfloat16
I32 = mybir.dt.int32
AX_X = mybir.AxisListType.X

P = 128
D = 2048
TP, NB, TS = 256, 8, 8
NS = NB * TS
T = TP + NS
KD = D // P
H, HKV, DH, GRP = 8, 2, 128, 4
HI, DI = 16, 64
PAST, PAGE = 2048, 128
NPG = PAST // PAGE
L = PAST + TS
DFF = 5504
KF = DFF // P
EPS = 1e-6
SCALE = DH ** -0.5
NEG = -1e30
TAKEN = -3e38
NBUCK = 32
RVEC = 512
RD0 = 255
C_QA, C_KI, C_QB, C_QC, C_GATE = 0, 2560, 2640, 4176, 10320
COLS = 256
KU = 8
O_A, O_B, O_C = 0, 8, 16
KF1 = 24
KF2 = KF - KF1


class Chain:

    def __init__(self, eng, sem):
        self.eng, self.sem, self.base, self.n = eng, sem, 0, 0

    def __call__(self, ins, apart=None):
        ins.then_inc(self.sem, 1)
        self.n += 1
        if apart:
            apart(self.eng, self.sem, self.base + self.n)
        else:
            self.eng.wait_ge(self.sem, self.base + self.n)

    @contextmanager
    def loop(self, start, end, per):
        b0 = self.base + self.n
        with self.eng.Fori(start, end) as i:
            self.base, self.n = b0 + (i - start) * per if start else b0 + i * per, 0
            yield i
            assert self.n == per, (self.n, per)
        self.base, self.n = b0 + (end - start) * per, 0


def build(nc, a, out):
    ctx = ExitStack()
    with ctx:
        def sem(name):
            return ctx.enter_context(nc.semaphore(name))

        def tensor(stack, name, shape, dt=F32):
            return stack.enter_context(nc.sbuf_tensor(name, shape, dt))

        o_scr = nc.dram_tensor("o_scr", [32, P, T], F32).ap()
        r_scr = nc.dram_tensor("r_scr", [16, RVEC], F32).ap()
        w_scr = nc.dram_tensor("w_scr", [HI, NS], F32).ap()

        dense = ctx.enter_context(nc.psum_tensor("dense", [P, 4, 512], F32))
        bank = [dense[:, i, :] for i in range(4)]
        bank += [ctx.enter_context(nc.psum_tensor(f"bank{i}", [P, 512], F32))[:, :] for i in range(4, 8)]
        ident = tensor(ctx, "ident", [P, P])
        ones = tensor(ctx, "ones", [P, P])
        epsc = tensor(ctx, "epsc", [P, 1])
        gmix = tensor(ctx, "gmix", [P, KD])
        gffn = tensor(ctx, "gffn", [P, KD])
        gfin = tensor(ctx, "gfin", [P, KD])
        rstd = tensor(ctx, "rstd", [P, T])
        pt_sb = tensor(ctx, "pt_sb", [1, NB * NPG], I32)
        h_hi = tensor(ctx, "h_hi", [P, KD, T], F32R)
        h_lo = tensor(ctx, "h_lo", [P, KD, T], F32R)
        w_raw = tensor(ctx, "w_raw", [P, 2, KU * COLS])
        w_hi = tensor(ctx, "w_hi", [P, 2, KU * COLS], F32R)
        w_lo = tensor(ctx, "w_lo", [P, 2, KU * COLS], F32R)

        with ExitStack() as st:
            xT0 = tensor(st, "xT0", [P, KD, T])
            tmp0 = tensor(st, "tmp0", [P, KD, T])
        with ExitStack() as st:
            zc = tensor(st, "zc", [P, 48, T])
            rotJ = tensor(st, "rotJ", [P, P])
            cosT = tensor(st, "cosT", [P, T])
            sinT = tensor(st, "sinT", [P, T])
            intraP = tensor(st, "intraP", [P, H, P])
            intraS = tensor(st, "intraS", [NS, H, NS])
            crossT = tensor(st, "crossT", [P, H, P])
            tailP = tensor(st, "tailP", [P, H])
            tailS = tensor(st, "tailS", [NS, H, NB])
            decay = tensor(st, "decay", [P, 2, H])
            retgn = tensor(st, "retgn", [P, 16])
            qr = tensor(st, "qr", [P, T])
            kr = tensor(st, "kr", [P, T])
            qx = tensor(st, "qx", [P, T])
            vcur = tensor(st, "vcur", [P, 2, T])
            vnP = tensor(st, "vnP", [P, 2, 256])
            vnS = tensor(st, "vnS", [NS, 256])
            knP = tensor(st, "knP", [P, 2, P])
            kexp = tensor(st, "kexp", [P, NB, P])
            attP = tensor(st, "attP", [P, 2, P])
            attS = tensor(st, "attS", [NS, NS])
            s_mid = tensor(st, "s_mid", [P, 256])
            s_fin = tensor(st, "s_fin", [P, 256])
            silu = tensor(st, "silu", [P, 2, T])
            state = tensor(st, "state", [P, 2, NB, 256])
        with ExitStack() as st:
            za = tensor(st, "za", [P, 21, T])
            vnat = tensor(st, "vnat", [P, 2, 256])
            kin = tensor(st, "kin", [P, 2, 80])
            wqb = tensor(st, "wqb", [80, NS])
            sel16 = tensor(st, "sel16", [P, 2, TP], BF16)
            m16 = tensor(st, "m16", [NS, L], BF16)
            oT = tensor(st, "oT", [P, H, T])
            near = tensor(st, "near", [NS, 2, 136])
            far = tensor(st, "far", [NS, 2])
            top8 = tensor(st, "top8", [P, 8])
            top8b = tensor(st, "top8b", [P, 8])
            identb = tensor(st, "identb", [P, P], BF16)
            with ExitStack() as s2:
                onehot = tensor(s2, "onehot", [NBUCK + 1, RVEC])
                tabx = tensor(s2, "tabx", [NBUCK + 1, 16])
                rvec = tensor(s2, "rvec", [16, RVEC])
                causP = tensor(s2, "causP", [P, 2, TP])
                causS = tensor(s2, "causS", [NS, TS])
                csel = tensor(s2, "csel", [P, NB, NS])
                ki2 = tensor(s2, "ki2", [P, T])
                qodd = tensor(s2, "qodd", [DI, 8, NS])
                qi64 = tensor(s2, "qi64", [DI, NB, HI, TS])
                wcol = tensor(s2, "wcol", [P, NB])
                wsel = tensor(s2, "wsel", [P, NB, NS])
                rel = tensor(s2, "rel", [P, 2, 512])
                accP = tensor(s2, "accP", [P, TP])
                kix = tensor(s2, "kix", [P, 4, 4, DI])
                kixT = tensor(s2, "kixT", [DI, 2, 512])
                score = tensor(s2, "score", [NS, L])
            with ExitStack() as s2:
                strip = tensor(s2, "strip", [P, H, 384])
                strip_rev = tensor(s2, "strip_rev", [P, H, 384])
                anti = tensor(s2, "anti", [P, P])
                lgP = tensor(s2, "lgP", [P, 2, TP])
                stP = tensor(s2, "stP", [P, 2, 4])
                pTP = tensor(s2, "pTP", [P, 2, TP])
            with ExitStack() as s2:
                kpg = tensor(s2, "kpg", [P, NPG, 256])
                vpg = tensor(s2, "vpg", [P, NPG, 256])
                kT = tensor(s2, "kT", [P, 2, 2, 512])
                lg = tensor(s2, "lg", [NS, L])
                pT = tensor(s2, "pT", [P, NPG, NS])
                pTn = tensor(s2, "pTn", [TS, NS])
                qcur = tensor(s2, "qcur", [P, H, TS])
                kvcur = tensor(s2, "kvcur", [P, 4, TS])
                vnew = tensor(s2, "vnew", [TS, 256])
                eall = tensor(s2, "eall", [NS, NB, NS])
                ecur = tensor(s2, "ecur", [NS, NS], BF16)
                stS = tensor(s2, "stS", [NS, 4])
                gate = tensor(s2, "gate", [NS, 16])
                gneg = tensor(s2, "gneg", [NS, 8])
        with ExitStack() as st:
            m_f = tensor(st, "m_f", [P, KD, T])
            with ExitStack() as s2:
                o_hi = tensor(s2, "o_hi", [P, 32, T], F32R)
                o_lo = tensor(s2, "o_lo", [P, 32, T], F32R)
                sig = tensor(s2, "sig", [P, 2, T])
                term = tensor(s2, "term", [P, 2, T])
                o_stage = tensor(s2, "o_stage", [P, 4, T])
            with ExitStack() as s2:
                m_hi = tensor(s2, "m_hi", [P, KD, T], F32R)
                m_lo = tensor(s2, "m_lo", [P, KD, T], F32R)
        with ExitStack() as st:
            x1 = tensor(st, "x1", [P, KD, T])
            y_hi = tensor(st, "y_hi", [P, KF1, T], F32R)
            y_lo = tensor(st, "y_lo", [P, KF1, T], F32R)
            cw = tensor(st, "cw", [P, 4, KF])
            ue = tensor(st, "ue", [P, 2, 338])
            cv = tensor(st, "cv", [P, 2, T])
            yv = tensor(st, "yv", [P, 2, T])
            cst = tensor(st, "cst", [P, KF, 16])
            cend = tensor(st, "cend", [P, KF, 18])
        with ExitStack() as st:
            x1b = tensor(st, "x1_again", [P, KD, T])
            tmp1 = tensor(st, "tmp1", [P, KD, T])

        w_arrived = [sem(f"w_arrived{i}") for i in range(2)]
        w_hi_done = sem("w_hi_done")
        w_split = sem("w_split")
        w_used = sem("w_used")
        bank_free = [sem(f"bank_free{i}") for i in range(2)]
        act_chain, dve_chain = sem("act_chain"), sem("dve_chain")
        phase_act, phase_dve, phase_pool = sem("phase_act"), sem("phase_dve"), sem("phase_pool")
        consts_in = sem("consts_in")
        x_arrived = sem("x_arrived")
        n_sq, n_sum, n_var, n_root, n_rstd = (sem("n_" + s) for s in ("sq", "sum", "var", "root", "rstd"))
        n_f, n_hi = sem("n_f"), sem("n_hi")
        stored = sem("stored")

        apart_n = sem("apart_n")

        def wait_apart(eng, sem_, value):
            eng.wait_ge(sem_, value)
            eng.sem_inc(apart_n, 1)

        c_att, c_fin, c_head, c_in, c_kn, c_mid = (
            sem(n) for n in ("c_att", "c_fin", "c_head", "c_in", "c_kn", "c_mid"))
        c_new, c_o, c_qk, c_root, c_rot, c_s = (
            sem(n) for n in ("c_new", "c_o", "c_qk", "c_root", "c_rot", "c_s"))
        c_silu, c_snew, c_sq, c_ss, c_turned, c_vcur = (
            sem(n) for n in ("c_silu", "c_snew", "c_sq", "c_ss", "c_turned", "c_vcur"))
        c_vn, cend_done, cv_made, cw_in, dn_relu, dn_s = (
            sem(n) for n in ("c_vn", "cend_done", "cv_made", "cw_in", "dn_relu", "dn_s"))
        dn_w, eall_in, ecur_done, eps_set, g_done, gate_done = (
            sem(n) for n in ("dn_w", "eall_in", "ecur_done", "eps_set", "g_done", "gate_done"))
        i_in, ix_relu, ix_s, ix_used, ki_in, kin_done = (
            sem(n) for n in ("i_in", "ix_relu", "ix_s", "ix_used", "ki_in", "kin_done"))
        kin_ps, kix_turned, kxT_done, kxT_used, m_hi_done, nat_done = (
            sem(n) for n in ("kin_ps", "kix_turned", "kxT_done", "kxT_used", "m_hi_done", "nat_done"))
        nat_ps, near_in, o_hi_done, o_in, o_split, pl_done = (
            sem(n) for n in ("nat_ps", "near_in", "o_hi_done", "o_in", "o_split", "pl_done"))
        pl_evac, pm_done, po_done, po_evac, pp_done, pt_evac = (
            sem(n) for n in ("pl_evac", "pm_done", "po_done", "po_evac", "pp_done", "pt_evac"))
        pt_ps, px_done, qi_ready, r_made, r_ps, rel_done = (
            sem(n) for n in ("pt_ps", "px_done", "qi_ready", "r_made", "r_ps", "rel_done"))
        rel_used, retp_out, sc_done, strip_evac, strip_in, strip_ps = (
            sem(n) for n in ("rel_used", "retp_out", "sc_done", "strip_evac", "strip_in", "strip_ps"))
        tabx_set, ue_done, ue_zero, x1_in, y_done, yh_done = (
            sem(n) for n in ("tabx_set", "ue_done", "ue_zero", "x1_in", "y_done", "yh_done"))
        ym_done = sem("ym_done")
        cur_done, ex_done, kT_act, kT_dve, k_turned, lg_act = (
            [sem(f"{n}{m}") for m in "ab"] for n in ("cur_done", "ex_done", "kT_act", "kT_dve", "k_turned", "lg_act"))
        lg_ps, mx_done, o_done, o_evac, pT_act, pT_dve = (
            [sem(f"{n}{m}") for m in "ab"] for n in ("lg_ps", "mx_done", "o_done", "o_evac", "pT_act", "pT_dve"))
        pT_ps, p_done, v_in, vnew_ps = (
            [sem(f"{n}{m}") for m in "ab"] for n in ("pT_ps", "p_done", "v_in", "vnew_ps"))
        k_in = [[sem(f"k_in{m}{i}") for i in range(4)] for m in "ab"]
        kix_in = [sem(f"kix_in{i}") for i in range(4)]
        state_in = [sem(f"state_in{i}") for i in range(2)]
        state_out = [sem(f"state_out{i}") for i in range(2)]
        N_CONST, N_CIN, N_IIN = 5, 10, 5
        NPOOL = a["cache_a_k"].shape[1]

        def wv(name):
            return a[name][0].rearrange("(k p) n -> p k n", p=P)

        W = {n: wv(n) for n in ("w_in", "w_pa", "w_pb", "w_pc", "w_out", "ffn_up", "ffn_gate", "ffn_down")}
        X = {"h": (h_hi, h_lo), "o": (o_hi, o_lo), "m": (m_hi, m_lo), "y": (y_hi, y_lo)}

        def job(w, col, src, xk=0, k=KD, wk=0, ncol=COLS):
            step = KU if ncol == COLS else KD
            return [(W[w], wk + k0, min(step, k - k0), col, ncol, src, xk + k0) for k0 in range(0, k, step)]

        def jobs_in(c0):
            return lambda i: [job("w_in", c0 + (2 * i + j) * COLS, "h") for j in range(2)]

        def jobs_merge(i):
            return [job("w_in", C_GATE + i * COLS, "h"), job("w_pa", i * COLS, "o", O_A, 8),
                    job("w_in", C_GATE + D + i * COLS, "h"), job("w_pb", i * COLS, "o", O_B, 8),
                    job("w_in", C_GATE + 2 * D + i * COLS, "h"), job("w_pc", i * COLS, "o", O_C, 16)]

        def jobs_out(i):
            return [job("w_out", (2 * i + j) * COLS, "m") for j in range(2)]

        def jobs_ff(b0):
            return lambda i: [job("ffn_up", b0 * P + i * COLS, "h"), job("ffn_gate", b0 * P + i * COLS, "h")]

        def jobs_down(b0, k):
            return lambda i: [job("ffn_down", (2 * i + j) * COLS, "y", 0, k, b0) for j in range(2)]

        STAGES, at_u, at_j = {}, 0, 0
        for name, n, fn in (
                ("C", 12, jobs_in(C_QC)), ("A", 5, jobs_in(C_QA)),
                ("KI", 1, lambda i: [job("w_in", C_KI, "h", ncol=P)]),
                ("B", 3, jobs_in(C_QB)), ("M", 8, jobs_merge), ("O", 4, jobs_out),
                ("F1", KF1 // 2, jobs_ff(0)), ("D1", 4, jobs_down(0, KF1)),
                ("F2", KF2 // 2, jobs_ff(KF1)),
                ("F3", 1, lambda i: [job(w, (KF - 1) * P, "h", ncol=P) for w in ("ffn_up", "ffn_gate")]),
                ("D2", 4, jobs_down(KF1, KF2))):
            nu, nj = sum(len(j) for j in fn(0)), len(fn(0))
            STAGES[name] = (n, fn, at_u, at_j, nu, nj)
            assert n == 1 or (nu % 2 == 0 and nj % 2 == 0)
            at_u, at_j = at_u + n * nu, at_j + n * nj

        def slot_of(w, slot, nk, ncol):
            return w[:, slot, 0:nk * ncol].rearrange("p (k n) -> p k n", k=nk)

        def sp_stage(sp, name):
            n, fn, u0, j0, nu, nj = STAGES[name]

            def body(i):
                for c, (w, k0, nk, col, ncol, _, _) in enumerate(x for j in fn(i) for x in j):
                    s = (u0 + c) % 2
                    if u0 + c >= 2 or not isinstance(i, int):
                        wait_apart(sp, w_split, u0 + i * nu + c - 1)
                    sp.dma_start(slot_of(w_raw, s, nk, ncol), w[:, k0:k0 + nk, bass.ds(col, ncol)])\
                        .then_inc(w_arrived[s], 16)

            first = 1 if u0 < 2 else 0
            if first or n == 1:
                body(0)
            if n > 1:
                with sp.Fori(first, n) as i:
                    body(i)

        def lagged(eng, chain, name, unit, evac, per):
            n, fn, u0, j0, nu, nj = STAGES[name]

            def body(i, first):
                c = 0
                for j, units in enumerate(fn(i)):
                    for (w, k0, nk, col, ncol, _, _) in units:
                        unit(u0 + i * nu + c, (u0 + c) % 2, nk * ncol, (u0 + c) // 2 + i * (nu // 2))
                        c += 1
                    if j or not first:
                        prev, ii = (j - 1, i) if j else (nj - 1, i - 1)
                        used = u0 + i * nu + c - len(units)
                        evac(prev, ii, (j0 + prev) % 2, used)
            body(0, True)
            if n > 1:
                with chain.loop(1, n, per) as i:
                    body(i, False)
            evac(nj - 1, n - 1, (j0 + nj - 1) % 2, u0 + n * nu)

        def act_stage(act, chain, name, evac, per=0):
            def unit(u, s, size, in_slot):
                act.wait_ge(w_arrived[s], 16 * (in_slot + 1))
                if not isinstance(u, int) or u >= 2:
                    act.wait_ge(w_used, u - 1)
                nc.scalar.activation(w_hi[:, s, 0:size], w_raw[:, s, 0:size], ACT.Copy).then_inc(w_hi_done, 1)
            lagged(act, chain, name, unit, evac, per)

        def dve_stage(dve, chain, name, evac, per=0):
            def unit(u, s, size, in_slot):
                dve.wait_ge(w_hi_done, u + 1)
                nc.vector.tensor_tensor(w_lo[:, s, 0:size], w_raw[:, s, 0:size],
                                        w_hi[:, s, 0:size].bitcast(F32), ALU.subtract).then_inc(w_split, 1)
            lagged(dve, chain, name, unit, evac, per)

        def pe_stage(pe, name):
            n, fn, u0, j0, nu, nj = STAGES[name]

            def body(i):
                c = 0
                for j, units in enumerate(fn(i)):
                    q = (j0 + j) % 2
                    if j0 + j >= 2 or not isinstance(i, int):
                        pe.wait_ge(bank_free[q], (j0 + j) // 2 + i * (nj // 2))
                    for m, (w, k0, nk, col, ncol, src, xk) in enumerate(units):
                        s = (u0 + c) % 2
                        xh, xl = X[src]
                        pe.wait_ge(w_split, u0 + i * nu + c + 1)
                        hi, lo = slot_of(w_hi, s, nk, ncol), slot_of(w_lo, s, nk, ncol)
                        for k in range(nk):
                            for b in range(ncol // P):
                                for t, (wp, xp) in enumerate(((hi, xh), (hi, xl), (lo, xh))):
                                    mm = nc.tensor.matmul(
                                        dense[:, 2 * q + b, 0:T], wp[:, k, b * P:(b + 1) * P], xp[:, xk + k, :],
                                        start=(m == 0 and k == 0 and t == 0),
                                        stop=(m == len(units) - 1 and k == nk - 1 and t == 2))
                        mm.then_inc(w_used, 1)
                        c += 1
            if n == 1:
                body(0)
            elif j0 < 2:
                body(0)
                with pe.Fori(1, n) as i:
                    body(i)
            else:
                with pe.Fori(0, n) as i:
                    body(i)

        block = ctx.enter_context(nc.Block())

        @block.sync
        def _(sp):
            def pages_index(c):
                for b in range(NB):
                    if not isinstance(c, int) or b >= 4:
                        wait_apart(sp, kix_turned, c * NB + b - 3)
                    for j in range(4):
                        page = sp.value_load(pt_sb[0:1, bass.ds(c * 4 + (b * NPG + j), 1)],
                                             min_val=0, max_val=NPOOL - 1)
                        sp.dma_start(kix[:, b % 4, j, :], a["cache_a_kidx"][0][bass.ds(page, 1), :, :]
                                     .rearrange("a p d -> (a p) d")).then_inc(kix_in[b % 4], 16)

            def pages_kv(mx, b):
                kc, vc = (("cache_a_k", "cache_a_v"), ("cache_b_k", "cache_b_v"))[mx]
                first = isinstance(b, int)
                for p in range(NPG):
                    if p % 4 == 0 and not first:
                        wait_apart(sp, k_turned[mx], b * 4 + p // 4 - 3)
                    page = sp.value_load(pt_sb[0:1, bass.ds(b * NPG + p, 1)], min_val=0, max_val=NPOOL - 1)
                    sp.dma_start(kpg[:, p, :], a[kc][0][bass.ds(page, 1), :, :, :]
                                 .rearrange("a p g d -> (a p) (g d)")).then_inc(k_in[mx][p // 4], 16)
                if not first:
                    wait_apart(sp, o_done[mx], b)
                for p in range(NPG):
                    page = sp.value_load(pt_sb[0:1, bass.ds(b * NPG + p, 1)], min_val=0, max_val=NPOOL - 1)
                    sp.dma_start(vpg[:, p, :], a[vc][0][bass.ds(page, 1), :, :, :]
                                 .rearrange("a p g d -> (a p) (g d)")).then_inc(v_in[mx], 16)

            sp_stage(sp, "C")
            sp_stage(sp, "A")
            sp_stage(sp, "KI")
            sp.wait_ge(consts_in, 16 * N_CONST)
            sp.wait_ge(phase_act, 3)
            sp.wait_ge(phase_dve, 3)
            sp.wait_ge(phase_pool, 3)
            pages_index(0)
            with sp.Fori(1, NPG // 4) as c:
                pages_index(c)
            for mx, ph in ((0, 6), (1, 9)):
                sp.wait_ge(phase_act, ph)
                sp.wait_ge(phase_dve, ph)
                pages_kv(mx, 0)
                with sp.Fori(1, NB) as b:
                    pages_kv(mx, b)
                if mx == 0:
                    sp_stage(sp, "B")
            for s in ("M", "O", "F1", "D1", "F2", "F3", "D2"):
                sp_stage(sp, s)

        @block.gpsimd
        def _(pool):
            def phase(k):
                pool.sem_inc(phase_pool, 1)
                pool.wait_ge(phase_act, k)
                pool.wait_ge(phase_dve, k)

            def load(dst, src, s):
                pool.dma_start(dst, src, allow_slow_non_contiguous=True).then_inc(s, 16)

            nst = [0]

            def store(dst, src):
                pool.dma_start(dst, src).then_inc(stored, 16)
                nst[0] += 1

            def stores_done():
                pool.wait_ge(stored, 16 * nst[0])

            load(ident[:, :], a["c_ident"], consts_in)
            for g, n in ((gmix, "norm_mix"), (gffn, "norm_ffn")):
                load(g[:, :], a[n], consts_in)
            load(gfin[:, :], a["norm_final"], consts_in)
            load(pt_sb[:, :], a["page_table"].rearrange("(o b) n -> o (b n)", o=1), consts_in)
            phase(1)
            for dst, n in ((rotJ, "c_rot"), (cosT, "c_cos"), (sinT, "c_sin"), (tailP, "c_tailp")):
                load(dst[:, :], a[n], c_in)
            for dst, n in ((intraP, "c_intrap"), (intraS, "c_intras"), (crossT, "c_cross"), (tailS, "c_tails"),
                           (decay, "c_decay")):
                load(dst[:, :, :], a[n], c_in)
            load(retgn[:, :], a["ret_gn"], c_in)

            def state_src(x, h):
                return x[0][:, bass.ds(h, 1), :, :].rearrange("b o d v -> d (b o) v")

            for s in range(2):
                load(state[:, s, :, :], state_src(a["state_ret"], s), state_in[s])
            phase(2)

            def head_out(i, more):
                for s in range(2):
                    h = 2 * i + s
                    pool.wait_ge(c_new, h + 1)
                    pool.dma_start(state_src(out["ret_s"], h), state[:, s, :, :]).then_inc(state_out[s], 16)
                    pool.dma_start(out["ret_p"][0, 0][bass.ds(h, 1), :, :].rearrange("o d v -> (o d) v"),
                                   s_fin[:, :]).then_inc(retp_out, 16)
                    if more:
                        pool.wait_ge(state_out[s], i * 16 + 16)
                        load(state[:, s, :, :], state_src(a["state_ret"], h + 2), state_in[s])
            with pool.Fori(0, H // 2 - 1) as i:
                head_out(i, True)
            head_out(H // 2 - 1, False)
            pool.wait_ge(state_out[0], 16 * H // 2)
            pool.wait_ge(state_out[1], 16 * H // 2)
            pool.wait_ge(retp_out, 16 * H)
            pool.wait_ge(c_head, H)
            store(o_scr[O_C:O_C + 16].rearrange("b p t -> p b t"), zc[:, 32:48, :])
            stores_done()
            phase(3)
            for dst, src in ((onehot[:, :], a["c_onehot"]), (tabx[0:NBUCK, :], a["rel_bias"]),
                             (causP[:, :, :], a["c_causp"]), (causS[:, :], a["c_causs"]),
                             (csel[:, :, :], a["c_sel"])):
                load(dst, src, i_in)
            pool.wait_ge(r_made, 1)
            store(r_scr, rvec[:, :])
            stores_done()
            for m in range(2):
                off = m * H * RVEC
                for q in range(TS):
                    load(near[q:NS:TS, m, :], bass.AP(r_scr.tensor, off + RD0 - PAGE - q, [[RVEC, H], [1, 136]]), near_in)
                load(far[:, m:m + 1], bass.AP(r_scr.tensor, off, [[RVEC, H], [0, TS], [1, 1]]), near_in)
            phase(4)
            load(ki2[0:DI, :], za[0:DI, 20, :], ki_in)
            load(ki2[DI:P, :], za[0:DI, 20, :], ki_in)
            load(qodd[:, :, :], za[DI:P, 12:20, TP:T], ki_in)
            store(w_scr, wqb[DI:DI + HI, :])
            stores_done()
            load(wcol[:, :], w_scr.rearrange("h (q b) -> (h q) b", b=NB), ki_in)

            store(out["kv_a"], za[:, 8:12, :])
            store(out["ki"], za[0:DI, 20, :])
            stores_done()
            phase(5)

            def attention(mx):
                load(strip_rev[:, :, :], bass.AP(r_scr.tensor, mx * H * RVEC, [[1, P], [RVEC, H], [1, 384]]), strip_in)
                load(anti[:, :], a["c_anti"], strip_in)
                phase(6 + 3 * mx)
                if mx == 0:
                    load(eall[:, :, :], a["c_eall"], eall_in)
                pool.wait_ge(o_evac[mx], NB)
                base = (O_A, O_B)[mx]
                store(o_scr[base:base + H].rearrange("b p t -> p b t"), oT[:, :, :])
                stores_done()
                phase(7 + 3 * mx)

            attention(0)
            phase(8)
            store(out["kv_b"], za[:, 8:12, :])
            attention(1)
            for g in range(8):
                if g >= 1:
                    pool.wait_ge(o_split, g)
                load(o_stage[:, :, :], o_scr[4 * g:4 * g + 4].rearrange("b p t -> p b t"), o_in)
            phase(11)
            phase(12)
            phase(13)
            load(x1[:, :, :], a["x"], x1_in)
            phase(14)
            phase(15)
            load(cw[:, 0:3, :], a["conv_w"], cw_in)
            load(cw[:, 3, :], a["conv_b"], cw_in)
            load(cst[:, :, :], a["state_conv"], cw_in)
            phase(16)
            pool.wait_ge(cend_done, KF // 2 + 1)
            store(out["conv_end"], cend[:, :, :])
            stores_done()
            phase(17)
            phase(18)
            pool.wait_ge(n_f, 12)
            store(out["y"], tmp1[:, :, :])
            stores_done()

        @block.tensor
        def _(pe):
            mmul, turn = nc.tensor.matmul, nc.tensor.transpose

            def phase(k):
                pe.wait_ge(phase_act, k)
                pe.wait_ge(phase_dve, k)

            def sums(src, r):
                pe.wait_ge(n_sq, r + 1)
                for k in range(KD):
                    mm = mmul(bank[4][:, 0:T], ones[:, :], src[:, k, :], start=(k == 0), stop=(k == KD - 1))
                mm.then_inc(n_sum, 1)

            pe.wait_ge(eps_set, 1)
            sums(tmp0, 0)
            phase(1)
            pe_stage(pe, "C")
            phase(2)
            pe.wait_ge(consts_in, 16 * N_CONST)
            pe.wait_ge(c_in, 16 * N_CIN)

            def retention(i):
                for s in range(2):
                    h = 2 * i + s
                    pe.wait_ge(c_head, h)
                    pe.wait_ge(c_new, h)
                    mmul(bank[4][:, 0:T], rotJ[:, :], zc[:, bass.ds(h, 1), :].rearrange("p o t -> p (o t)"),
                         start=True, stop=True)
                    mmul(bank[5][:, 0:T], rotJ[:, :], zc[:, bass.ds(h + 8, 1), :].rearrange("p o t -> p (o t)"),
                         start=True, stop=True).then_inc(c_rot, 1)
                    pe.wait_ge(c_qk, h + 1)
                    pe.wait_ge(c_vcur, h + 1)
                    for c in range(2):
                        turn(bank[6][:, c * P:(c + 1) * P], kr[:, c * P:(c + 1) * P], ident[:, :])
                    turn(bank[6][0:NS, 256:384], kr[:, TP:T], ident[:, :])
                    for b in range(2):
                        for c in range(2):
                            turn(bank[4][:, c * 256 + b * P:c * 256 + (b + 1) * P], vcur[:, b, c * P:(c + 1) * P],
                                 ident[:, :])
                        mm = turn(bank[5][0:NS, b * P:(b + 1) * P], vcur[:, b, TP:T], ident[:, :])
                    mm.then_inc(c_turned, 1)
                    for c in range(2):
                        mmul(bank[7][:, c * P:(c + 1) * P], kr[:, c * P:(c + 1) * P], qr[:, c * P:(c + 1) * P],
                             start=True, stop=True)
                    mmul(bank[7][0:NS, 256:320], kr[:, TP:T], qr[:, TP:T], start=True, stop=True).then_inc(c_att, 1)
                    pe.wait_ge(c_kn, h + 1)
                    pe.wait_ge(c_vn, h + 1)
                    for c in range(2):
                        mm = mmul(bank[6][:, c * 256:(c + 1) * 256], knP[:, c, :], vnP[:, c, :], start=True, stop=True)
                    mm.then_inc(c_s, 1)
                    pe.wait_ge(c_mid, h + 1)
                    pe.wait_ge(state_in[s], i * 16 + 16)
                    for b in range(2):
                        o, cb = bank[4 + b], slice(b * P, (b + 1) * P)
                        mmul(o[:, 0:P], vnP[:, 0, cb], attP[:, 0, :], start=True, stop=True)
                        mmul(o[:, P:TP], vnP[:, 1, cb], attP[:, 1, :], start=True, stop=False)
                        mmul(o[:, P:TP], s_mid[:, cb], qx[:, P:TP], start=False, stop=True)
                        mmul(o[:, TP:T], vnS[:, cb], attS[:, :], start=True, stop=True)
                        for r in range(NB):
                            c = slice(TP + r * TS, TP + (r + 1) * TS)
                            mm = mmul(o[:, c], state[:, s, r, cb], qx[:, c], start=False, stop=True,
                                      skip_group_check=True)
                    mm.then_inc(c_o, 1)
                    for r in range(NB):
                        mm = mmul(bank[r // 2][:, (r % 2) * 256:(r % 2 + 1) * 256], kexp[0:NS, r, :], vnS[:, :],
                                  start=True, stop=True)
                    mm.then_inc(c_snew, 1)
                    pe.wait_ge(c_sq, h + 1)
                    pe.wait_ge(c_fin, h + 1)
                    for b in range(2):
                        mm = mmul(bank[6][:, 0:T], ones[:, :], vcur[:, b, :], start=(b == 0), stop=(b == 1))
                    mm.then_inc(c_ss, 1)

            with pe.Fori(0, H // 2) as i:
                retention(i)
            phase(3)

            pe.wait_ge(i_in, 16 * N_IIN)
            pe.wait_ge(tabx_set, 1)
            mmul(bank[4][0:16, :], tabx[:, :], onehot[:, :], start=True, stop=True).then_inc(r_ps, 1)
            pe_stage(pe, "A")
            pe_stage(pe, "KI")
            phase(4)

            def natural(mx):
                for t in range(2):
                    for j in range(2):
                        mm = turn(bank[4 + t][:, j * P:(j + 1) * P], za[:, 10 + j, t * P:(t + 1) * P], ident[:, :])
                    mm.then_inc(nat_ps, 1)

            natural(0)
            for t in range(2):
                mm = turn(bank[7][:, t * 80:(t + 1) * 80], za[0:80, 20, t * P:(t + 1) * P], ident[0:80, 0:80])
            mm.then_inc(kin_ps, 1)
            pe.wait_ge(ki_in, 64)
            n = 0
            for t in range(2):
                for hp in range(HI // 2):
                    if n >= 2:
                        pe.wait_ge(ix_relu, n - 1)
                    for o in range(2):
                        rows = slice(o * DI, (o + 1) * DI)
                        mm = mmul(bank[2 * (n % 2) + o][:, 0:TP], za[rows, 12 + hp, t * P:(t + 1) * P],
                                  ki2[rows, 0:TP], start=True, stop=True)
                        mm.then_inc(ix_s, 1)
                    n += 1
            pe.wait_ge(qi_ready, 1)
            pe.wait_ge(nat_done, 2)
            for b in range(NB):
                mm = mmul(bank[6][:, b * TS:(b + 1) * TS], qi64[:, b, :, :].rearrange("p h q -> p (h q)"),
                          ki2[0:DI, TP + b * TS:TP + (b + 1) * TS], start=True, stop=True)
            mm.then_inc(dn_s, 1)
            pe.wait_ge(dn_relu, 1)
            for b in range(NB):
                mm = mmul(bank[3][0:NS, 0:TS], wsel[:, b, :], rel[:, 0, b * TS:(b + 1) * TS],
                          start=(b == 0), stop=(b == NB - 1))
            mm.then_inc(dn_w, 1)

            def index_chunk(c):
                first = isinstance(c, int)
                for st in range(NB + 2):
                    if st < NB:
                        b = st
                        if not first or b >= 2:
                            pe.wait_ge(kxT_used, c * NB + b - 1)
                        wait_apart(pe, kix_in[b % 4], c * 128 + (b // 4) * 64 + 64)
                        for j in range(4):
                            mm = turn(bank[4 + b % 2][0:DI, j * P:(j + 1) * P], kix[:, b % 4, j, :], ident[:, :])
                        mm.then_inc(kix_turned, 1)
                    if 1 <= st <= NB:
                        b = st - 1
                        pe.wait_ge(kxT_done, c * NB + b + 1)
                        if not first or b >= 2:
                            pe.wait_ge(rel_used, c * NB + b - 1)
                        else:
                            pe.wait_ge(dn_w, 1)
                        mmul(bank[6 + b % 2][:, :], qi64[:, b, :, :].rearrange("p h q -> p (h q)"),
                             kixT[:, b % 2, :], start=True, stop=True).then_inc(kxT_used, 1)
                    if st >= 2:
                        b = st - 2
                        pe.wait_ge(rel_done, c * NB + b + 1)
                        if b == 0 and not first:
                            pe.wait_ge(sc_done, c)
                        mmul(bank[2][0:NS, :], wsel[:, b, :], rel[:, b % 2, :], start=(b == 0), stop=(b == NB - 1))\
                            .then_inc(rel_used, 1)
            index_chunk(0)
            with pe.Fori(1, NPG // 4) as c:
                index_chunk(c)
            phase(5)

            def attention(mx):
                N = 2 * H
                pe.wait_ge(strip_in, 32 * (mx + 1))
                for h in range(H):
                    if h >= 4:
                        pe.wait_ge(strip_evac, mx * H + h - 3)
                    mmul(bank[h % 4][:, 0:384], anti[:, :], strip_rev[:, h, :], start=True, stop=True)\
                        .then_inc(strip_ps, 1)
                pe.wait_ge(strip_evac, mx * H + H)
                pe.wait_ge(nat_done, 2 * mx + 2)
                for n in range(N + 1):
                    if n < N:
                        t, h = n // H, n % H
                        nk = (t + 1) * P
                        if n >= 2:
                            pe.wait_ge(pl_evac, mx * 2 * H + n - 1)
                        mm = mmul(bank[n % 2][:, 0:nk], za[:, h, t * P:(t + 1) * P], za[:, 8 + h // GRP, 0:nk],
                                  start=True, stop=(mx == 1))
                        if mx == 0:
                            mm = mmul(bank[n % 2][:, 0:nk], identb[:, :], sel16[:, t, 0:nk], start=False, stop=True)
                        mm.then_inc(pl_done, 1)
                    if n >= 1:
                        m = n - 1
                        t, h = m // H, m % H
                        pe.wait_ge(pp_done, mx * 2 * H + m + 1)
                        for kt in range(t + 1):
                            mm = turn(bank[4 + m % 2][:, kt * P:(kt + 1) * P], lgP[:, m % 2, kt * P:(kt + 1) * P],
                                      ident[:, :])
                        mm.then_inc(pt_ps, 1)
                        pe.wait_ge(pt_evac, mx * 2 * H + m + 1)
                        if m >= 2:
                            pe.wait_ge(po_evac, mx * 2 * H + m - 1)
                        g = h // GRP
                        for kt in range(t + 1):
                            mm = mmul(bank[6 + m % 2][:, 0:P], vnat[:, kt, g * P:(g + 1) * P],
                                      pTP[:, m % 2, kt * P:(kt + 1) * P], start=(kt == 0), stop=(kt == t))
                        mm.then_inc(po_done, 1)
                phase(6 + 3 * mx)

                def decode(b):
                    first = isinstance(b, int)
                    pe.wait_ge(cur_done[mx], b + 1)
                    if mx == 0:
                        pe.wait_ge(ecur_done, b + 1)
                    for g in range(2):
                        mm = turn(bank[7][0:TS, g * P:(g + 1) * P], kvcur[:, 2 + g, :], ident[:, :])
                    mm.then_inc(vnew_ps[mx], 1)
                    for st in range(5):
                        if st < 4:
                            pe.wait_ge(k_in[mx][st], b * 64 + 64)
                            if not first or st >= 1:
                                pe.wait_ge(kT_act[mx], b * 4 + st)
                                pe.wait_ge(kT_dve[mx], b * 4 + st)
                            for g in range(2):
                                for j in range(4):
                                    mm = turn(bank[4 + g][:, j * P:(j + 1) * P], kpg[:, 4 * st + j, g * P:(g + 1) * P],
                                              ident[:, :])
                            mm.then_inc(k_turned[mx], 1)
                        if st >= 1:
                            c = st - 1
                            pe.wait_ge(kT_act[mx], b * 4 + c + 1)
                            pe.wait_ge(kT_dve[mx], b * 4 + c + 1)
                            if c == 0 and not first:
                                pe.wait_ge(o_evac[mx], b)
                            for g in range(2):
                                mm = mmul(bank[c][g * 32:(g + 1) * 32, :],
                                          qcur[:, g * GRP:(g + 1) * GRP, :].rearrange("p r q -> p (r q)"),
                                          kT[:, c % 2, g, :], start=True, stop=True)
                            if mx == 0:
                                mm = mmul(bank[c][0:NS, :], ecur[:, :], m16[:, c * 512:(c + 1) * 512],
                                          start=False, stop=True, skip_group_check=True)
                            mm.then_inc(lg_ps[mx], 1)
                    for g in range(2):
                        mm = mmul(bank[6][g * 32:(g + 1) * 32, 0:TS],
                                  qcur[:, g * GRP:(g + 1) * GRP, :].rearrange("p r q -> p (r q)"),
                                  kvcur[:, g, :], start=True, stop=True)
                    if mx == 0:
                        mm = mmul(bank[6][0:NS, 0:TS], ecur[:, :], m16[:, PAST:L], start=False, stop=True,
                                  skip_group_check=True)
                    mm.then_inc(lg_ps[mx], 1)
                    wait_apart(pe, p_done[mx], b + 1)
                    for p in range(NPG):
                        mm = turn(bank[p // 8][:, (p % 8) * NS:(p % 8 + 1) * NS], lg[:, p * P:(p + 1) * P],
                                  ident[0:NS, 0:NS])
                    turn(bank[2][0:TS, 0:NS], lg[:, PAST:L], ident[0:NS, 0:NS]).then_inc(pT_ps[mx], 1)
                    pe.wait_ge(pT_act[mx], b + 1)
                    pe.wait_ge(pT_dve[mx], b + 1)
                    pe.wait_ge(v_in[mx], b * 256 + 256)
                    for g in range(2):
                        cols = slice(g * 32, (g + 1) * 32)
                        for p in range(NPG):
                            mmul(bank[3][:, cols], vpg[:, p, g * P:(g + 1) * P], pT[:, p, cols], start=(p == 0), stop=False)
                        mm = mmul(bank[3][:, cols], vnew[:, g * P:(g + 1) * P], pTn[:, cols], start=False, stop=True)
                    mm.then_inc(o_done[mx], 1)
                decode(0)
                with pe.Fori(1, NB) as b:
                    decode(b)
                phase(7 + 3 * mx)

            attention(0)
            pe_stage(pe, "B")
            phase(8)
            natural(1)
            attention(1)
            phase(11)
            pe_stage(pe, "M")
            phase(13)
            pe_stage(pe, "O")
            phase(14)
            sums(tmp1, 1)
            phase(15)

            pe_stage(pe, "F1")
            phase(16)
            pe_stage(pe, "D1")
            pe_stage(pe, "F2")
            pe_stage(pe, "F3")
            phase(17)
            pe_stage(pe, "D2")
            phase(18)
            sums(tmp1, 2)

        def evacuated(eng, name):
            n, fn, u0, j0, nu, nj = STAGES[name]
            done = j0 + n * nj
            eng.wait_ge(bank_free[0], (done + 1) // 2)
            if done > 1:
                eng.wait_ge(bank_free[1], done // 2)

        @block.scalar
        def _(act):
            A = Chain(act, act_chain)
            fn = nc.scalar.activation

            def phase(k):
                act.sem_inc(phase_act, 1)
                act.wait_ge(phase_dve, k)
                act.wait_ge(phase_pool, k)

            def norm(src, tmp, r, split):
                fn(tmp[:, :, :], src[:, :, :], ACT.Square).then_inc(n_sq, 1)
                act.wait_ge(n_sum, r + 1)
                fn(rstd[:, :], bank[4][:, 0:T], ACT.Sqrt, bias=epsc[:, :], scale=1.0 / D).then_inc(n_root, 1)
                if split:
                    for g in range(4):
                        act.wait_ge(n_f, 4 * r + g + 1)
                        ks = slice(4 * g, 4 * g + 4)
                        fn(h_hi[:, ks, :], tmp[:, ks, :], ACT.Copy).then_inc(n_hi, 1)

            for g in range(2):
                ks = slice(8 * g, 8 * g + 8)
                act.dma_start(xT0[:, ks, :], a["x"][:, ks, :]).then_inc(x_arrived, 16)
            act.wait_ge(x_arrived, 32)
            act.wait_ge(eps_set, 1)
            norm(xT0, tmp0, 0, True)
            act.wait_ge(n_hi, 4)
            phase(1)

            def to_blocks(dst):
                def evac(j, i, q, used):
                    act.wait_ge(w_used, used)
                    fn(dst[:, bass.ds(4 * i + 2 * j, 2), :], dense[:, 2 * q:2 * q + 2, 0:T], ACT.Copy)\
                        .then_inc(bank_free[q], 1)
                return evac

            act_stage(act, A, "C", to_blocks(zc))
            evacuated(act, "C")
            phase(2)

            def retention(i):
                for s in range(2):
                    h = 2 * i + s
                    act.wait_ge(c_head, h)
                    act.wait_ge(c_new, h)
                    fn(vcur[:, :, :], zc[:, bass.ds(2 * h + 16, 2), :], ACT.Copy).then_inc(c_vcur, 1)
                    fn(silu[:, :, :], zc[:, bass.ds(2 * h + 32, 2), :], ACT.Silu).then_inc(c_silu, 1)
                    act.wait_ge(c_turned, h + 1)
                    fn(vnP[:, :, :].rearrange("p c v -> p (c v)"), bank[4], ACT.Copy)
                    fn(vnS[:, :], bank[5][0:NS, 0:256], ACT.Copy).then_inc(c_vn, 1)
                    act.wait_ge(c_s, h + 1)
                    fn(s_mid[:, :], bank[6][:, 0:256], ACT.Copy).then_inc(c_mid, 1)
                    act.wait_ge(c_o, h + 1)
                    for b in range(2):
                        ins = fn(vcur[:, b, :], bank[4 + b][:, 0:T], ACT.Square)
                    ins.then_inc(c_sq, 1)
                    act.wait_ge(c_ss, h + 1)
                    fn(rstd[:, :], bank[6][:, 0:T], ACT.Sqrt, bias=epsc[:, :], scale=1.0 / 256).then_inc(c_root, 1)
            with act.Fori(0, H // 2) as i:
                retention(i)
            phase(3)
            act.wait_ge(r_ps, 1)
            fn(rvec[:, :], bank[4][0:16, :], ACT.Copy).then_inc(r_made, 1)
            act_stage(act, A, "A", to_blocks(za))

            def ki_block(j, i, q, used):
                act.wait_ge(w_used, used)
                fn(za[:, 20, :], dense[:, 2 * q, 0:T], ACT.Copy).then_inc(bank_free[q], 1)
            act_stage(act, A, "KI", ki_block)
            evacuated(act, "KI")
            act.wait_ge(r_made, 1)
            A(fn(wqb[DI:DI + HI, :].rearrange("h (q b) -> h q b", b=NB),
                 za[DI:DI + HI, 20, TP:T].rearrange("h (b q) -> h q b", q=TS), ACT.Copy))
            phase(4)

            def scale_and_natural(mx):
                A(fn(za[:, 0:H, :], za[:, 0:H, :], ACT.Copy, scale=SCALE))
                for t in range(2):
                    act.wait_ge(nat_ps, 2 * mx + t + 1)
                    fn(vnat[:, t, :], bank[4 + t][:, 0:256], ACT.Copy).then_inc(nat_done, 1)
                act.wait_ge(nat_done, 2 * mx + 2)

            scale_and_natural(0)
            act.wait_ge(kin_ps, 1)
            for t in range(2):
                fn(kin[:, t, :], bank[7][:, t * 80:(t + 1) * 80], ACT.Copy).then_inc(kin_done, 1)
            A(fn(identb[:, :], ident[:, :], ACT.Copy))
            rs = (DI * HI) ** -0.5
            for n in range(HI):
                act.wait_ge(ix_s, 2 * n + 2)
                if n >= 2:
                    act.wait_ge(ix_used, n - 1)
                fn(rel[:, n % 2, :].rearrange("p (o k) -> p o k", o=2),
                   dense[:, 2 * (n % 2):2 * (n % 2) + 2, 0:TP], ACT.Relu, scale=rs).then_inc(ix_relu, 1)
            act.wait_ge(ix_used, HI)
            act.wait_ge(dn_s, 1)
            fn(rel[:, 0, 0:NS], bank[6][:, 0:NS], ACT.Relu, scale=rs).then_inc(dn_relu, 1)
            act.wait_ge(dn_w, 1)

            def index_chunk(c):
                for st in range(NB + 1):
                    if st < NB:
                        b = st
                        act.wait_ge(kix_turned, c * NB + b + 1)
                        fn(kixT[:, b % 2, :], bank[4 + b % 2][0:DI, :], ACT.Copy).then_inc(kxT_done, 1)
                    if st >= 1:
                        b = st - 1
                        act.wait_ge(kxT_used, c * NB + b + 1)
                        if not isinstance(c, int) or b >= 2:
                            act.wait_ge(rel_used, c * NB + b - 1)
                        fn(rel[:, b % 2, :], bank[6 + b % 2], ACT.Relu, scale=rs).then_inc(rel_done, 1)
            index_chunk(0)
            with act.Fori(1, NPG // 4) as c:
                index_chunk(c)
            phase(5)

            def attention(mx):
                N = 2 * H
                for n in range(N + 2):
                    if n < N:
                        nk = (n // H + 1) * P
                        act.wait_ge(pm_done, mx * 2 * H + n + 1)
                        fn(lgP[:, n % 2, 0:nk], lgP[:, n % 2, 0:nk], ACT.Exp, bias=stP[:, n % 2, 1:2],
                           accum_out=stP[:, n % 2, 2:3]).then_inc(px_done, 1)
                    if 1 <= n <= N:
                        m = n - 1
                        nk = (m // H + 1) * P
                        act.wait_ge(pt_ps, mx * 2 * H + m + 1)
                        if m >= 2:
                            act.wait_ge(po_done, mx * 2 * H + m - 1)
                        fn(pTP[:, m % 2, 0:nk], bank[4 + m % 2][:, 0:nk], ACT.Copy).then_inc(pt_evac, 1)
                    if n >= 2:
                        m = n - 2
                        t, h = m // H, m % H
                        act.wait_ge(po_done, mx * 2 * H + m + 1)
                        fn(oT[:, h, t * P:(t + 1) * P], bank[6 + m % 2][:, 0:P], ACT.Copy).then_inc(po_evac, 1)
                act.wait_ge(po_evac, mx * 2 * H + N)
                phase(6 + 3 * mx)

                def decode(b):
                    cols = bass.ds(b * TS + TP, TS)
                    act.wait_ge(o_done[mx], b)
                    fn(qcur[:, :, :], za[:, 0:H, cols], ACT.Copy)
                    fn(kvcur[:, :, :], za[:, H:H + 4, cols], ACT.Copy).then_inc(cur_done[mx], 1)
                    act.wait_ge(vnew_ps[mx], b + 1)
                    A(fn(vnew[:, :], bank[7][0:TS, 0:256], ACT.Copy))
                    for st in range(5):
                        if st < 4:
                            act.wait_ge(k_turned[mx], b * 4 + st + 1)
                            fn(kT[:, st % 2, 0, :], bank[4], ACT.Copy).then_inc(kT_act[mx], 1)
                        if 1 <= st < 4:
                            c = st - 1
                            act.wait_ge(lg_ps[mx], b * 5 + c + 1)
                            if mx == 1:
                                act.wait_ge(gate_done, b * 4 + c + 1)
                            fn(lg[:, c * 512:(c + 1) * 512], bank[c][0:NS, :], ACT.Identity, bias=far[:, mx:mx + 1])\
                                .then_inc(lg_act[mx], 1)
                    act.wait_ge(mx_done[mx], b + 1)
                    fn(lg[:, :], lg[:, :], ACT.Exp, bias=stS[:, 1:2], accum_out=stS[:, 2:3]).then_inc(ex_done[mx], 1)
                    act.wait_ge(pT_ps[mx], b + 1)
                    fn(pT[:, 0:8, :].rearrange("p k q -> p (k q)"), bank[0], ACT.Copy).then_inc(pT_act[mx], 1)
                    act.wait_ge(o_done[mx], b + 1)
                    fn(oT[:, :, cols], bank[3][:, 0:NS].rearrange("p (h q) -> p h q", q=TS), ACT.Copy)\
                        .then_inc(o_evac[mx], 1)
                act.wait_ge(near_in, 16 * 2 * (TS + 1))
                with A.loop(0, NB, 1) as b:
                    decode(b)
                act.wait_ge(o_evac[mx], NB)
                phase(7 + 3 * mx)

            attention(0)
            act_stage(act, A, "B", to_blocks(za))
            evacuated(act, "B")
            phase(8)
            scale_and_natural(1)
            attention(1)
            for g in range(8):
                act.wait_ge(o_in, 16 * (g + 1))
                fn(o_hi[:, 4 * g:4 * g + 4, :], o_stage[:, :, :], ACT.Copy).then_inc(o_hi_done, 1)
            act.wait_ge(o_hi_done, 8)
            phase(11)
            mj0 = STAGES["M"][3]

            def gates(j, i, q, used):
                if j % 2 == 0:
                    act.wait_ge(w_used, used)
                    act.wait_ge(bank_free[1 - q], (mj0 + j - 1) // 2 + 3 * i + 1)
                    fn(sig[:, :, :], dense[:, 2 * q:2 * q + 2, 0:T], ACT.Sigmoid).then_inc(bank_free[q], 1)
            act_stage(act, A, "M", gates)
            evacuated(act, "M")
            phase(12)
            fn(m_hi[:, :, :], m_f[:, :, :], ACT.Copy).then_inc(m_hi_done, 1)
            act.wait_ge(m_hi_done, 1)
            phase(13)
            act_stage(act, A, "O", lambda j, i, q, used: None)
            phase(14)
            norm(x1, tmp1, 1, True)
            act.wait_ge(n_hi, 8)
            phase(15)

            def ff(base, yb, nb):
                def evac(j, i, q, used):
                    n = base + i
                    if j == 0:
                        act.wait_ge(w_used, used)
                        act.wait_ge(cv_made, n)
                        fn(ue[:, 0:nb, 2:2 + TP], dense[:, 2 * q:2 * q + nb, 0:TP], ACT.Copy)
                        for b in range(nb):
                            ins = fn(ue[:, b, 258:338].rearrange("p (r t) -> p r t", t=10)[:, :, 2:10],
                                     dense[:, 2 * q + b, TP:T].rearrange("p (r t) -> p r t", t=TS), ACT.Copy)
                        ins.then_inc(bank_free[q], 1)
                        for b in range(nb):
                            ins = fn(ue[:, b, 258:338].rearrange("p (r t) -> p r t", t=10)[:, :, 0:2],
                                     cst[:, bass.ds(2 * n + b, 1), :].rearrange("p o (r t) -> p (o r) t", t=2), ACT.Copy)
                        ins.then_inc(ue_done, 1)
                        act.wait_ge(ue_done, n + 1)
                        f2 = bass.ds(2 * n, nb)
                        fn(cend[:, f2, 0:2], ue[:, 0:nb, 256:258], ACT.Copy)
                        for b in range(nb):
                            ins = fn(cend[:, bass.ds(2 * n + b, 1), 2:18].rearrange("p o (r t) -> p (o r) t", t=2),
                                     ue[:, b, 258:338].rearrange("p (r t) -> p r t", t=10)[:, :, 8:10], ACT.Copy)
                        ins.then_inc(cend_done, 1)
                    else:
                        act.wait_ge(cv_made, n + 1)
                        act.wait_ge(y_done, n)
                        fn(yv[:, 0:nb, :], cv[:, 0:nb, :], ACT.Gelu).then_inc(g_done, 1)
                        act.wait_ge(ym_done, n + 1)
                        fn(y_hi[:, bass.ds(yb + 2 * i, nb), :], yv[:, 0:nb, :], ACT.Copy).then_inc(yh_done, 1)
                return evac
            act.wait_ge(cw_in, 48)
            act_stage(act, A, "F1", ff(0, 0, 2))
            act.wait_ge(yh_done, KF1 // 2)
            phase(16)
            act_stage(act, A, "D1", lambda j, i, q, used: None)
            act_stage(act, A, "F2", ff(KF1 // 2, 0, 2))
            act_stage(act, A, "F3", ff(KF // 2, KF2 - 1, 1))
            act.wait_ge(yh_done, KF // 2 + 1)
            phase(17)
            act_stage(act, A, "D2", lambda j, i, q, used: None)
            phase(18)
            norm(x1, tmp1, 2, False)

        @block.vector
        def _(dve):
            V = Chain(dve, dve_chain)
            tt, stt, ts = nc.vector.tensor_tensor, nc.vector.scalar_tensor_tensor, nc.vector.tensor_scalar
            copy = nc.vector.tensor_copy

            def phase(k):
                dve.sem_inc(phase_dve, 1)
                dve.wait_ge(phase_act, k)
                dve.wait_ge(phase_pool, k)

            def norm(src, tmp, g, r, split):
                dve.wait_ge(n_root, r + 1)
                V(nc.vector.reciprocal(rstd[:, :], rstd[:, :]))
                for k in range(KD):
                    ins = stt(tmp[:, k, :], src[:, k, :], g[:, k:k + 1], rstd[:, :], ALU.mult, ALU.mult)
                    if k % 4 == 3:
                        ins.then_inc(n_f, 1)
                dve.wait_ge(n_f, 4 * r + 4)
                if split:
                    for q in range(4):
                        dve.wait_ge(n_hi, 4 * r + q + 1)
                        ks = slice(4 * q, 4 * q + 4)
                        V(tt(h_lo[:, ks, :], tmp[:, ks, :], h_hi[:, ks, :].bitcast(F32), ALU.subtract))

            nc.vector.memset(epsc[:, :], EPS)
            nc.vector.memset(ones[:, :], 1.0).then_inc(eps_set, 1)
            dve.wait_ge(consts_in, 16 * N_CONST)
            norm(xT0, tmp0, gmix, 0, True)
            phase(1)

            def nothing(j, i, q, used):
                pass
            dve_stage(dve, V, "C", nothing)
            phase(2)
            dve.wait_ge(c_in, 16 * N_CIN)

            def retention(i):
                for s in range(2):
                    h = 2 * i + s

                    def blk(x, n=1):
                        v = zc[:, bass.ds(x, n), :]
                        return v.rearrange("p o t -> p (o t)") if n == 1 else v
                    dve.wait_ge(c_rot, h + 1)
                    V(tt(qr[:, :], blk(h), cosT[:, :], ALU.mult))
                    V(tt(qx[:, :], bank[4][:, 0:T], sinT[:, :], ALU.mult))
                    V(tt(qr[:, :], qr[:, :], qx[:, :], ALU.add))
                    V(stt(kr[:, :], blk(h + 8), SCALE, cosT[:, :], ALU.mult, ALU.mult))
                    V(stt(qx[:, :], bank[5][:, 0:T], SCALE, sinT[:, :], ALU.mult, ALU.mult))
                    ins = tt(kr[:, :], kr[:, :], qx[:, :], ALU.add)
                    ins.then_inc(c_qk, 1)
                    dve.wait_ge(c_qk, h + 1)
                    cr = crossT[:, bass.ds(h, 1), :].rearrange("p o t -> p (o t)")
                    V(tt(qx[:, P:TP], qr[:, P:TP], cr, ALU.mult))
                    V(tt(qx[:, TP:T].rearrange("p (r t) -> p r t", t=TS), qr[:, TP:T].rearrange("p (r t) -> p r t", t=TS),
                         cr[:, 0:TS].unsqueeze(1).to_broadcast([P, NB, TS]), ALU.mult))
                    dve.wait_ge(c_turned, h + 1)
                    V(ts(knP[:, :, :].rearrange("p c d -> p (c d)"), bank[6][:, 0:256], tailP[:, bass.ds(h, 1)], None,
                         ALU.mult))
                    V(tt(kexp[0:NS, :, :], bank[6][0:NS, 256:384].unsqueeze(1).to_broadcast([NS, NB, P]),
                         tailS[:, bass.ds(h, 1), :].rearrange("p o r -> p (o r)").unsqueeze(2).to_broadcast([NS, NB, P]),
                         ALU.mult))
                    dve.wait_ge(c_att, h + 1)
                    V(tt(attP[:, :, :], bank[7][:, 0:256].rearrange("p (c q) -> p c q", c=2),
                         intraP[:, bass.ds(h, 1), :].to_broadcast([P, 2, P]), ALU.mult))
                    ins = tt(attS[:, :], bank[7][0:NS, 256:320],
                             intraS[:, bass.ds(h, 1), :].rearrange("p o q -> p (o q)"), ALU.mult)
                    ins.then_inc(c_kn, 1)
                    dve.wait_ge(c_mid, h + 1)
                    dve.wait_ge(retp_out, h * 16)
                    stt(s_fin[:, :], s_mid[:, :], decay[:, 0, bass.ds(h, 1)], bank[6][:, 256:512],
                        ALU.mult, ALU.add).then_inc(c_fin, 1)
                    dve.wait_ge(c_fin, h + 1)
                    dve.wait_ge(c_snew, h + 1)
                    st_h = state[:, s, :, :].rearrange("p r v -> p (r v)")
                    stt(st_h, st_h, decay[:, 1, bass.ds(h, 1)], dense[:, :, :].rearrange("p b v -> p (b v)"),
                        ALU.mult, ALU.add).then_inc(c_new, 1)
                    dve.wait_ge(c_root, h + 1)
                    V(nc.vector.reciprocal(rstd[:, :], rstd[:, :]))
                    dve.wait_ge(c_silu, h + 1)
                    for b in range(2):
                        V(stt(blk(2 * h + 32 + b), bank[4 + b][:, 0:T], retgn[:, bass.ds(2 * h + b, 1)], rstd[:, :],
                              ALU.mult, ALU.mult))
                    tt(blk(2 * h + 32, 2), blk(2 * h + 32, 2), silu[:, :, :], ALU.mult).then_inc(c_head, 1)
                    dve.wait_ge(c_head, h + 1)
            with V.loop(0, H // 2, 2 * 13) as i:
                retention(i)
            dve.wait_ge(c_new, H)
            phase(3)
            nc.vector.memset(tabx[NBUCK:NBUCK + 1, :], NEG).then_inc(tabx_set, 1)
            dve.wait_ge(tabx_set, 1)
            dve_stage(dve, V, "A", nothing)
            dve_stage(dve, V, "KI", nothing)
            phase(4)
            dve.wait_ge(ki_in, 64)
            q_src = za[0:DI, 12:20, TP:T].rearrange("p j (b q) -> p b j q", q=TS)
            V(tt(wsel[:, :, :], csel[:, :, :], wcol[:, :].unsqueeze(2).to_broadcast([P, NB, NS]), ALU.mult))
            for b in range(NB):
                cs = slice(b * TS, (b + 1) * TS)
                V(copy(qi64[:, b, 0:HI:2, :], za[0:DI, 12:20, TP + b * TS:TP + (b + 1) * TS]))
                V(copy(qi64[:, b, 1:HI:2, :], qodd[:, :, cs]))
            dve.sem_inc(qi_ready, 1)
            dve.wait_ge(kin_done, 2)

            def take8(vals, rows, best):
                V(nc.vector.max(best[0:rows, :], vals), wait_apart)
                V(nc.vector.match_replace(vals, best[0:rows, :], vals, TAKEN), wait_apart)

            n = 0
            for t in range(2):
                for hp in range(HI // 2):
                    dve.wait_ge(ix_relu, n + 1)
                    for o in range(2):
                        h = 2 * hp + o
                        ins = stt(accP[:, :], rel[:, n % 2, o * TP:(o + 1) * TP], kin[:, t, DI + h:DI + h + 1],
                                  causP[:, t, :] if h == 0 else accP[:, :], ALU.mult, ALU.add)
                        if o == 0:
                            V(ins)
                    n += 1
                    ins.then_inc(ix_used, 1)
                    dve.wait_ge(ix_used, n)
                with V.loop(0, TP // 4 // 8, 2):
                    take8(accP[:, :], P, top8)
                V(ts(sel16[:, t, :], accP[:, :], TAKEN, NEG, ALU.not_equal, ALU.mult))
            dve.wait_ge(dn_w, 1)
            V(tt(score[:, PAST:L], bank[3][0:NS, 0:TS], causS[:, :], ALU.add))
            with dve.Fori(0, NPG // 4) as c:
                dve.wait_ge(rel_used, c * NB + NB)
                copy(score[:, bass.ds(c * 512, 512)], bank[2][0:NS, :]).then_inc(sc_done, 1)
            dve.wait_ge(sc_done, NPG // 4)
            with V.loop(0, 256 // 8, 2):
                take8(score[:, :], NS, top8b)
            V(ts(m16[:, :], score[:, :], TAKEN, NEG, ALU.not_equal, ALU.mult))
            phase(5)

            def attention(mx):
                N = 2 * H
                for h in range(H):
                    dve.wait_ge(strip_ps, mx * H + h + 1)
                    copy(strip[:, h, :], bank[h % 4][:, 0:384]).then_inc(strip_evac, 1)
                dve.wait_ge(strip_evac, mx * H + H)
                for n in range(N + 1):
                    if n < N:
                        t, h = n // H, n % H
                        nk = (t + 1) * P
                        off = P - t * P
                        dve.wait_ge(pl_done, mx * 2 * H + n + 1)
                        if n >= 2:
                            dve.wait_ge(pt_ps, mx * 2 * H + n - 1)
                        tt(lgP[:, n % 2, 0:nk], bank[n % 2][:, 0:nk], strip[:, h, off:off + nk], ALU.add)\
                            .then_inc(pl_evac, 1)
                        dve.wait_ge(pl_evac, mx * 2 * H + n + 1)
                        V(nc.vector.tensor_reduce(stP[:, n % 2, 0:1], lgP[:, n % 2, 0:nk], AX_X, ALU.max))
                        ts(stP[:, n % 2, 1:2], stP[:, n % 2, 0:1], -1.0, None, ALU.mult).then_inc(pm_done, 1)
                    if n >= 1:
                        m = n - 1
                        nk = (m // H + 1) * P
                        dve.wait_ge(px_done, mx * 2 * H + m + 1)
                        V(nc.vector.reciprocal(stP[:, m % 2, 3:4], stP[:, m % 2, 2:3]))
                        ts(lgP[:, m % 2, 0:nk], lgP[:, m % 2, 0:nk], stP[:, m % 2, 3:4], None, ALU.mult)\
                            .then_inc(pp_done, 1)
                dve.wait_ge(pp_done, mx * 2 * H + N)
                phase(6 + 3 * mx)

                def decode(b):
                    dve.wait_ge(o_done[mx], b)
                    if mx == 0:
                        copy(ecur[:, :], eall[:, bass.ds(b, 1), :].rearrange("p o r -> p (o r)")).then_inc(ecur_done, 1)

                    def gate_sum(c):
                        nc.vector.tensor_reduce(gate[:, 2 * c:2 * c + 2],
                                                bank[c][0:NS, :].rearrange("p (o k) -> p o k", o=2), AX_X, ALU.add)\
                            .then_inc(gate_done, 1)
                    for st in range(4):
                        dve.wait_ge(k_turned[mx], b * 4 + st + 1)
                        copy(kT[:, st % 2, 1, :], bank[5]).then_inc(kT_dve[mx], 1)
                        if mx == 1 and st >= 1:
                            dve.wait_ge(lg_ps[mx], b * 5 + st)
                            gate_sum(st - 1)
                    dve.wait_ge(lg_ps[mx], b * 5 + 4)
                    if mx == 1:
                        gate_sum(3)
                    V(ts(lg[:, PAST - 512:PAST - P], bank[3][0:NS, 0:384], far[:, mx:mx + 1], None, ALU.add))
                    V(tt(lg[:, PAST - P:PAST], bank[3][0:NS, 384:512], near[:, mx, 0:P], ALU.add))
                    dve.wait_ge(lg_ps[mx], b * 5 + 5)
                    V(tt(lg[:, PAST:L], bank[6][0:NS, 0:TS], near[:, mx, P:P + TS], ALU.add))
                    dve.wait_ge(lg_act[mx], b * 3 + 3)
                    if mx == 1:
                        dve.wait_ge(gate_done, b * 4 + 4)
                        V(nc.vector.memset(gate[:, 8:13], -TAKEN))
                        V(nc.vector.memset(gate[:, 13:16], NEG), wait_apart)
                        take8(gate[:, :], NS, top8b)
                        V(ts(gneg[:, :], gate[:, 0:8], TAKEN, NEG, ALU.not_equal, ALU.mult))
                        past = lg[:, 0:PAST].rearrange("p (o k) -> p o k", o=8)
                        V(tt(past, past, gneg[:, :].unsqueeze(2).to_broadcast([NS, 8, 256]), ALU.add))
                    V(nc.vector.tensor_reduce(stS[:, 0:1], lg[:, :], AX_X, ALU.max))
                    ts(stS[:, 1:2], stS[:, 0:1], -1.0, None, ALU.mult).then_inc(mx_done[mx], 1)
                    dve.wait_ge(ex_done[mx], b + 1)
                    V(nc.vector.reciprocal(stS[:, 3:4], stS[:, 2:3]))
                    ts(lg[:, :], lg[:, :], stS[:, 3:4], None, ALU.mult).then_inc(p_done[mx], 1)
                    dve.wait_ge(pT_ps[mx], b + 1)
                    copy(pT[:, 8:16, :].rearrange("p k q -> p (k q)"), bank[1])
                    copy(pTn[:, :], bank[2][0:TS, 0:NS]).then_inc(pT_dve[mx], 1)
                if mx == 0:
                    dve.wait_ge(eall_in, 16)
                dve.wait_ge(near_in, 16 * 2 * (TS + 1))
                with V.loop(0, NB, 5 if mx == 0 else 11) as b:
                    decode(b)
                dve.wait_ge(pT_dve[mx], NB)
                phase(7 + 3 * mx)

            attention(0)
            dve_stage(dve, V, "B", nothing)
            phase(8)
            attention(1)
            for g in range(8):
                dve.wait_ge(o_hi_done, g + 1)
                gs = slice(4 * g, 4 * g + 4)
                tt(o_lo[:, gs, :], o_stage[:, :, :], o_hi[:, gs, :].bitcast(F32), ALU.subtract).then_inc(o_split, 1)
            dve.wait_ge(o_split, 8)
            phase(11)
            mj0 = STAGES["M"][3]

            def merge(j, i, q, used):
                if j % 2 == 0:
                    return
                dve.wait_ge(w_used, used)
                dve.wait_ge(bank_free[1 - q], (mj0 + j - 1) // 2 + 3 * i + 1)
                m2 = m_f[:, bass.ds(2 * i, 2), :]
                nth = (mj0 + j) // 2 + 3 * i + 1
                tt(m2 if j == 1 else term[:, :, :], sig[:, :, :], dense[:, 2 * q:2 * q + 2, 0:T], ALU.mult)\
                    .then_inc(bank_free[q], 1)
                dve.wait_ge(bank_free[q], nth)
                if j > 1:
                    V(tt(m2, m2, term[:, :, :], ALU.add))
            dve_stage(dve, V, "M", merge, 2)
            evacuated(dve, "M")
            phase(12)
            dve.wait_ge(m_hi_done, 1)
            V(tt(m_lo[:, :, :], m_f[:, :, :], m_hi[:, :, :].bitcast(F32), ALU.subtract))
            phase(13)

            def into_x1(j, i, q, used):
                dve.wait_ge(w_used, used)
                x2 = x1[:, bass.ds(4 * i + 2 * j, 2), :]
                tt(x2, x2, dense[:, 2 * q:2 * q + 2, 0:T], ALU.add).then_inc(bank_free[q], 1)
            dve.wait_ge(x1_in, 16)
            dve_stage(dve, V, "O", into_x1)
            evacuated(dve, "O")
            phase(14)
            norm(x1, tmp1, gffn, 1, True)
            phase(15)
            dve.wait_ge(cw_in, 48)
            nc.vector.memset(ue[:, :, 0:2], 0.0).then_inc(ue_zero, 1)

            def ff(base, yb, nb):
                def evac(j, i, q, used):
                    n = base + i
                    if j == 0:
                        dve.wait_ge(ue_done, n + 1)
                        dve.wait_ge(g_done, n)
                        for b in range(nb):
                            f = 2 * n + b
                            src = (lambda k: ue[:, b, k:k + TP],
                                   lambda k: ue[:, b, 258:338].rearrange("p (r t) -> p r t", t=10)[:, :, k:k + TS])
                            dst = (cv[:, b, 0:TP], cv[:, b, TP:T].rearrange("p (r t) -> p r t", t=TS))

                            def w(k):
                                return cw[:, k, bass.ds(f, 1)]
                            for r in range(2):
                                ins = ts(dst[r], src[r](0), w(0), w(3), ALU.mult, ALU.add)
                            V(ins)
                            for k in (1, 2):
                                for r in range(2):
                                    ins = stt(dst[r], src[r](k), w(k), dst[r], ALU.mult, ALU.add)
                                if k == 1 or b < nb - 1:
                                    V(ins)
                        ins.then_inc(cv_made, 1)
                    else:
                        dve.wait_ge(w_used, used)
                        dve.wait_ge(g_done, n + 1)
                        nth = (STAGES["F1"][3] + 1) // 2
                        y2 = yv[:, 0:nb, :]
                        V(tt(y2, y2, dense[:, 2 * q:2 * q + nb, 0:T], ALU.mult))
                        dve.sem_inc(bank_free[q], 1)
                        dve.sem_inc(ym_done, 1)
                        dve.wait_ge(yh_done, n + 1)
                        yb2 = bass.ds(yb + 2 * i, nb)
                        tt(y_lo[:, yb2, :], y2, y_hi[:, yb2, :].bitcast(F32), ALU.subtract).then_inc(y_done, 1)
                return evac
            dve_stage(dve, V, "F1", ff(0, 0, 2), 6)
            dve.wait_ge(y_done, KF1 // 2)
            phase(16)
            dve_stage(dve, V, "D1", into_x1)
            dve_stage(dve, V, "F2", ff(KF1 // 2, 0, 2), 6)
            dve_stage(dve, V, "F3", ff(KF // 2, KF2 - 1, 1))
            dve.wait_ge(y_done, KF // 2 + 1)
            phase(17)
            dve_stage(dve, V, "D2", into_x1)
            evacuated(dve, "D2")
            phase(18)
            norm(x1, tmp1, gfin, 2, False)


def constants():
    f = np.float32
    c = {"c_ident": np.eye(P, dtype=f), "c_anti": np.eye(P, dtype=f)[::-1]}
    rot = np.zeros((P, P), f)
    for m in range(64):
        rot[m + 64, m] = -1
        rot[m, m + 64] = 1
    c["c_rot"] = rot
    pos = np.concatenate([np.arange(TP), np.tile(PAST + np.arange(TS), NB)]).astype(f)
    inv = f(10000.0) ** (-np.arange(0, DH, 2, dtype=f) / f(DH))
    ang = pos[None, :] * inv[:, None].astype(f)
    c["c_cos"] = np.concatenate([np.cos(ang)] * 2).astype(f)
    c["c_sin"] = np.concatenate([np.sin(ang)] * 2).astype(f)
    lg = np.log1p(-np.exp2(-5.0 - np.arange(H)))
    i = np.arange(P, dtype=np.float64)
    diff = i[None, :] - i[:, None]
    c["c_intrap"] = np.where(diff[:, None, :] >= 0, np.exp(np.maximum(diff, 0)[:, None, :] * lg[None, :, None]), 0).astype(f)
    r, q = np.arange(NS) // TS, np.arange(NS) % TS
    d8 = q[None, :] - q[:, None]
    ok = (r[None, :] == r[:, None]) & (d8 >= 0)
    c["c_intras"] = np.where(ok[:, None, :], np.exp(np.maximum(d8, 0)[:, None, :] * lg[None, :, None]), 0).astype(f)
    c["c_cross"] = np.broadcast_to(np.exp((i + 1)[None, :] * lg[:, None]), (P, H, P)).astype(f)
    c["c_tailp"] = np.exp((P - 1 - i)[:, None] * lg[None, :]).astype(f)
    c["c_tails"] = (np.exp((TS - 1 - q)[:, None, None] * lg[None, :, None])
                    * (r[:, None, None] == np.arange(NB)[None, None, :])).astype(f)
    c["c_decay"] = np.broadcast_to(np.exp(np.array([P, TS])[:, None] * lg[None, :]), (P, 2, H)).astype(f)
    dist = RD0 - np.arange(RVEC)
    n = np.maximum(dist, 0)
    half = NBUCK // 2
    nf = np.maximum(n, 1).astype(f)
    large = half + (np.log(nf / f(half)) / f(np.log(128 / half)) * f(NBUCK - half)).astype(np.int32)
    bucket = np.where(n < half, n, np.minimum(large, NBUCK - 1))
    one = np.zeros((NBUCK + 1, RVEC), f)
    one[np.where(dist < 0, NBUCK, bucket), np.arange(RVEC)] = 1
    c["c_onehot"] = one
    k = np.arange(TP)
    qpos = np.arange(P)[:, None] + P * np.arange(2)[None, :]
    c["c_causp"] = np.where(k[None, None, :] <= qpos[:, :, None], 0, NEG).astype(f)
    c["c_causs"] = np.where(np.arange(TS)[None, :] <= q[:, None], 0, NEG).astype(f)
    hq = np.arange(P) % TS
    c["c_sel"] = ((r[None, None, :] == np.arange(NB)[None, :, None]) & (q[None, None, :] == hq[:, None, None])).astype(f)
    c["c_eall"] = ((r[:, None, None] == np.arange(NB)[None, :, None]) & (q[:, None, None] == q[None, None, :])).astype(f)
    return {n: np.ascontiguousarray(v) for n, v in c.items()}


_INS = ['cache_a_k', 'cache_a_v', 'cache_a_kidx', 'cache_b_k', 'cache_b_v', 'state_ret', 'page_table', 'rel_bias',
        'w_in', 'w_pa', 'w_pb', 'w_pc', 'w_out', 'ffn_up', 'ffn_gate', 'ffn_down']
_OUTS = [("y", (P, KD, T)), ("kv_a", (P, 4, T)), ("ki", (DI, T)), ("kv_b", (P, 4, T)),
         ("ret_p", (1, 1, H, DH, 256)), ("ret_s", (1, NB, H, DH, 256)), ("conv_end", (P, KF, 18))]


def lay_in(x):
    def features(v):
        v = np.asarray(v)
        return v.reshape(v.shape[0], -1, P).transpose(2, 1, 0)

    def blocks(v):
        return features(np.asarray(v).reshape(1, -1))[:, :, 0]

    return {
        "x": features(np.concatenate([np.asarray(x["x_prompt"])[0], np.asarray(x["x_sample"]).reshape(NS, D)])),
        "norm_mix": blocks(x["norm_mix"]), "norm_ffn": blocks(x["norm_ffn"]), "norm_final": blocks(x["norm_final"]),
        "ret_gn": blocks(x["ret_gn"]), "conv_b": blocks(x["conv_b"]),
        "conv_w": features(np.asarray(x["conv_w"])[0]).transpose(0, 2, 1),
        "state_conv": features(np.asarray(x["state_conv"]).reshape(2 * NB, DFF)),
    }


def lay_out(r):
    def rows(v):
        return v.transpose(2, 1, 0).reshape(v.shape[2], -1)

    y, end, ki = rows(r["y"]), rows(r["conv_end"]), r["ki"].T
    kv = []
    for m in "ab":
        v = rows(r["kv_" + m]).reshape(T, 2, HKV, DH)
        kv.append([v[:TP, 0][None, None], v[:TP, 1][None, None],
                   v[TP:, 0].reshape(1, NB, TS, HKV, DH), v[TP:, 1].reshape(1, NB, TS, HKV, DH)])
    (akp, avp, aks, avs), (bkp, bvp, bks, bvs) = kv
    return (y[:TP][None], y[TP:].reshape(NB, TS, D), akp, avp, ki[:TP][None, None], bkp, bvp, r["ret_p"],
            end[:2][None, None], aks, avs, ki[TP:].reshape(1, NB, TS, DI), bks, bvs, r["ret_s"],
            end[2:].reshape(1, NB, 2, DFF))


def kernel(**inputs):
    import concourse.bacc as _bacc
    from concourse.bass_utils import run_bass_kernel_spmd as _run

    nc = _bacc.Bacc("TRN2", target_bir_lowering=False, num_devices=1)
    arrays, a, out = {}, {}, {}
    for name, x in [(n, inputs[n]) for n in _INS] + sorted(lay_in(inputs).items()) + sorted(constants().items()):
        x = np.ascontiguousarray(x)
        arrays[f"in_{name}"] = x
        a[name] = nc.dram_tensor(f"in_{name}", x.shape, mybir.dt.from_np(x.dtype), kind="ExternalInput").ap()
    for name, shape in _OUTS:
        out[name] = nc.dram_tensor(f"out_{name}", shape, F32, kind="ExternalOutput").ap()
    build(nc, a, out)
    r = _run(nc, [arrays], core_ids=[0])
    return tuple(np.ascontiguousarray(v) for v in lay_out({n: r.results[0][f"out_{n}"] for n, _ in _OUTS}))
```

```python
from contextlib import ExitStack, contextmanager

import numpy as np

import concourse.bass as bass
from concourse import mybir

ALU = mybir.AluOpType
ACT = mybir.ActivationFunctionType
F32 = mybir.dt.float32
F32R = mybir.dt.float32r
BF16 = mybir.dt.bfloat16
I32 = mybir.dt.int32
AX_X = mybir.AxisListType.X

P = 128
D = 2048
TP, NB, TS = 256, 8, 8
NS = NB * TS
T = TP + NS
KD = D // P
H, HKV, DH, GRP = 8, 2, 128, 4
HI, DI = 16, 64
PAST, PAGE = 2048, 128
NPG = PAST // PAGE
L = PAST + TS
DFF = 5504
KF = DFF // P
EPS = 1e-6
SCALE = DH ** -0.5
NEG = -1e30
TAKEN = -3e38
NBUCK = 32
RVEC = 512
RD0 = 255
C_QA, C_KI, C_QB, C_QC, C_GATE = 0, 2560, 2640, 4176, 10320
COLS = 256
KU = 8
O_A, O_B, O_C = 0, 8, 16
KF1 = 24
KF2 = KF - KF1


class Chain:

    def __init__(self, eng, sem):
        self.eng, self.sem, self.base, self.n = eng, sem, 0, 0

    def __call__(self, ins, apart=None):
        ins.then_inc(self.sem, 1)
        self.n += 1
        if apart:
            apart(self.eng, self.sem, self.base + self.n)
        else:
            self.eng.wait_ge(self.sem, self.base + self.n)

    @contextmanager
    def loop(self, start, end, per):
        b0 = self.base + self.n
        with self.eng.Fori(start, end) as i:
            self.base, self.n = b0 + (i - start) * per if start else b0 + i * per, 0
            yield i
            assert self.n == per, (self.n, per)
        self.base, self.n = b0 + (end - start) * per, 0


def build(nc, a, out):
    ctx = ExitStack()
    with ctx:
        def sem(name):
            return ctx.enter_context(nc.semaphore(name))

        def tensor(stack, name, shape, dt=F32):
            return stack.enter_context(nc.sbuf_tensor(name, shape, dt))

        o_scr = nc.dram_tensor("o_scr", [32, P, T], F32).ap()
        r_scr = nc.dram_tensor("r_scr", [16, RVEC], F32).ap()
        w_scr = nc.dram_tensor("w_scr", [HI, NS], F32).ap()

        dense = ctx.enter_context(nc.psum_tensor("dense", [P, 4, 512], F32))
        bank = [dense[:, i, :] for i in range(4)]
        bank += [ctx.enter_context(nc.psum_tensor(f"bank{i}", [P, 512], F32))[:, :] for i in range(4, 8)]
        ident = tensor(ctx, "ident", [P, P])
        ones = tensor(ctx, "ones", [P, P])
        epsc = tensor(ctx, "epsc", [P, 1])
        gmix = tensor(ctx, "gmix", [P, KD])
        gffn = tensor(ctx, "gffn", [P, KD])
        gfin = tensor(ctx, "gfin", [P, KD])
        rstd = tensor(ctx, "rstd", [P, T])
        pt_sb = tensor(ctx, "pt_sb", [1, NB * NPG], I32)
        h_hi = tensor(ctx, "h_hi", [P, KD, T], F32R)
        h_lo = tensor(ctx, "h_lo", [P, KD, T], F32R)
        w_raw = tensor(ctx, "w_raw", [P, 2, KU * COLS])
        w_hi = tensor(ctx, "w_hi", [P, 2, KU * COLS], F32R)
        w_lo = tensor(ctx, "w_lo", [P, 2, KU * COLS], F32R)

        with ExitStack() as st:
            xT0 = tensor(st, "xT0", [P, KD, T])
            tmp0 = tensor(st, "tmp0", [P, KD, T])
        with ExitStack() as st:
            zc = tensor(st, "zc", [P, 48, T])
            rotJ = tensor(st, "rotJ", [P, P])
            cosT = tensor(st, "cosT", [P, T])
            sinT = tensor(st, "sinT", [P, T])
            intraP = tensor(st, "intraP", [P, H, P])
            intraS = tensor(st, "intraS", [NS, H, NS])
            crossT = tensor(st, "crossT", [P, H, P])
            tailP = tensor(st, "tailP", [P, H])
            tailS = tensor(st, "tailS", [NS, H, NB])
            decay = tensor(st, "decay", [P, 2, H])
            retgn = tensor(st, "retgn", [P, 16])
            qr = tensor(st, "qr", [P, T])
            kr = tensor(st, "kr", [P, T])
            qx = tensor(st, "qx", [P, T])
            vcur = tensor(st, "vcur", [P, 2, T])
            vnP = tensor(st, "vnP", [P, 2, 256])
            vnS = tensor(st, "vnS", [NS, 256])
            knP = tensor(st, "knP", [P, 2, P])
            kexp = tensor(st, "kexp", [P, NB, P])
            attP = tensor(st, "attP", [P, 2, P])
            attS = tensor(st, "attS", [NS, NS])
            s_mid = tensor(st, "s_mid", [P, 256])
            s_fin = tensor(st, "s_fin", [P, 256])
            silu = tensor(st, "silu", [P, 2, T])
            state = tensor(st, "state", [P, 2, NB, 256])
        with ExitStack() as st:
            za = tensor(st, "za", [P, 21, T])
            vnat = tensor(st, "vnat", [P, 2, 256])
            kin = tensor(st, "kin", [P, 2, 80])
            wqb = tensor(st, "wqb", [80, NS])
            sel16 = tensor(st, "sel16", [P, 2, TP], BF16)
            m16 = tensor(st, "m16", [NS, L], BF16)
            oT = tensor(st, "oT", [P, H, T])
            near = tensor(st, "near", [NS, 2, 136])
            far = tensor(st, "far", [NS, 2])
            top8 = tensor(st, "top8", [P, 8])
            top8b = tensor(st, "top8b", [P, 8])
            identb = tensor(st, "identb", [P, P], BF16)
            with ExitStack() as s2:
                onehot = tensor(s2, "onehot", [NBUCK + 1, RVEC])
                tabx = tensor(s2, "tabx", [NBUCK + 1, 16])
                rvec = tensor(s2, "rvec", [16, RVEC])
                causP = tensor(s2, "causP", [P, 2, TP])
                causS = tensor(s2, "causS", [NS, TS])
                csel = tensor(s2, "csel", [P, NB, NS])
                ki2 = tensor(s2, "ki2", [P, T])
                qodd = tensor(s2, "qodd", [DI, 8, NS])
                qi64 = tensor(s2, "qi64", [DI, NB, HI, TS])
                wcol = tensor(s2, "wcol", [P, NB])
                wsel = tensor(s2, "wsel", [P, NB, NS])
                rel = tensor(s2, "rel", [P, 2, 512])
                accP = tensor(s2, "accP", [P, TP])
                kixT = tensor(s2, "kixT", [DI, 4, 4, PAGE])
                score = tensor(s2, "score", [NS, L])
            with ExitStack() as s2:
                strip = tensor(s2, "strip", [P, H, 384])
                strip_rev = tensor(s2, "strip_rev", [P, H, 384])
                anti = tensor(s2, "anti", [P, P])
                lgP = tensor(s2, "lgP", [P, 2, TP])
                stP = tensor(s2, "stP", [P, 2, 4])
                pTP = tensor(s2, "pTP", [P, 2, TP])
            with ExitStack() as s2:
                kpg = tensor(s2, "kpg", [P, NPG, 2, PAGE])
                vpg = tensor(s2, "vpg", [P, NPG, 256])
                lg = tensor(s2, "lg", [NS, 2, L])
                pT = tensor(s2, "pT", [P, NPG, NS])
                pTn = tensor(s2, "pTn", [TS, NS])
                qcur = tensor(s2, "qcur", [P, 2, H, TS])
                kvcur = tensor(s2, "kvcur", [P, 2, 4, TS])
                vnew = tensor(s2, "vnew", [TS, 2, 256])
                eall = tensor(s2, "eall", [NS, NB, NS])
                ecur = tensor(s2, "ecur", [NS, 2, NS], BF16)
                stS = tensor(s2, "stS", [NS, 2, 4])
                gate = tensor(s2, "gate", [NS, 16])
                gneg = tensor(s2, "gneg", [NS, 8])
        with ExitStack() as st:
            m_f = tensor(st, "m_f", [P, KD, T])
            with ExitStack() as s2:
                o_hi = tensor(s2, "o_hi", [P, 32, T], F32R)
                o_lo = tensor(s2, "o_lo", [P, 32, T], F32R)
                sig = tensor(s2, "sig", [P, 2, T])
                term = tensor(s2, "term", [P, 2, T])
                o_stage = tensor(s2, "o_stage", [P, 2, 4, T])
            with ExitStack() as s2:
                m_hi = tensor(s2, "m_hi", [P, KD, T], F32R)
                m_lo = tensor(s2, "m_lo", [P, KD, T], F32R)
        with ExitStack() as st:
            x1 = tensor(st, "x1", [P, KD, T])
            y_hi = tensor(st, "y_hi", [P, KF1, T], F32R)
            y_lo = tensor(st, "y_lo", [P, KF1, T], F32R)
            cw = tensor(st, "cw", [P, 4, KF])
            ue = tensor(st, "ue", [P, 2, 338])
            cv = tensor(st, "cv", [P, 2, T])
            yv = tensor(st, "yv", [P, 2, T])
            cst = tensor(st, "cst", [P, KF, 16])
            cend = tensor(st, "cend", [P, KF, 18])
        with ExitStack() as st:
            x1b = tensor(st, "x1_again", [P, KD, T])
            tmp1 = tensor(st, "tmp1", [P, KD, T])

        w_arrived = [sem(f"w_arrived{i}") for i in range(2)]
        w_hi_done = sem("w_hi_done")
        w_split = sem("w_split")
        w_used = sem("w_used")
        bank_free = [sem(f"bank_free{i}") for i in range(2)]
        act_chain, dve_chain = sem("act_chain"), sem("dve_chain")
        phase_act, phase_dve, phase_pool = sem("phase_act"), sem("phase_dve"), sem("phase_pool")
        consts_in = sem("consts_in")
        x_arrived = sem("x_arrived")
        n_sq, n_sum, n_var, n_root, n_rstd = (sem("n_" + s) for s in ("sq", "sum", "var", "root", "rstd"))
        n_f, n_hi = sem("n_f"), sem("n_hi")
        stored = sem("stored")

        apart_n = sem("apart_n")

        def wait_apart(eng, sem_, value):
            eng.wait_ge(sem_, value)
            eng.sem_inc(apart_n, 1)

        c_att, c_fin, c_head, c_in, c_kn, c_mid = (
            sem(n) for n in ("c_att", "c_fin", "c_head", "c_in", "c_kn", "c_mid"))
        c_new, c_o, c_qk, c_root, c_rot, c_s = (
            sem(n) for n in ("c_new", "c_o", "c_qk", "c_root", "c_rot", "c_s"))
        c_silu, c_snew, c_sq, c_ss, c_turned, c_vcur = (
            sem(n) for n in ("c_silu", "c_snew", "c_sq", "c_ss", "c_turned", "c_vcur"))
        c_vn, cend_done, cv_made, cw_in, dn_relu, dn_s = (
            sem(n) for n in ("c_vn", "cend_done", "cv_made", "cw_in", "dn_relu", "dn_s"))
        dn_w, eall_in, ecur_done, eps_set, g_done, gate_done = (
            sem(n) for n in ("dn_w", "eall_in", "ecur_done", "eps_set", "g_done", "gate_done"))
        i_in, ix_relu, ix_s, ix_used, ki_in, kin_done = (
            sem(n) for n in ("i_in", "ix_relu", "ix_s", "ix_used", "ki_in", "kin_done"))
        kin_ps, kxT_used, m_hi_done, nat_done, nat_ps, near_in = (
            sem(n) for n in ("kin_ps", "kxT_used", "m_hi_done", "nat_done", "nat_ps", "near_in"))
        o_hi_done, o_split, pl_done, pl_evac, pm_done, po_done = (
            sem(n) for n in ("o_hi_done", "o_split", "pl_done", "pl_evac", "pm_done", "po_done"))
        po_evac, pp_done, pt_evac, pt_ps, px_done, qi_ready = (
            sem(n) for n in ("po_evac", "pp_done", "pt_evac", "pt_ps", "px_done", "qi_ready"))
        r_made, r_ps, rel_done, rel_used, retp_out, sc_done = (
            sem(n) for n in ("r_made", "r_ps", "rel_done", "rel_used", "retp_out", "sc_done"))
        sems, strip_evac, strip_in, strip_ps, tabx_set, ue_done = (
            sem(n) for n in ("sems", "strip_evac", "strip_in", "strip_ps", "tabx_set", "ue_done"))
        ue_zero, x1_in, y_done, yh_done, ym_done = (
            sem(n) for n in ("ue_zero", "x1_in", "y_done", "yh_done", "ym_done"))
        cur_done, ex_done, lg_act, lg_ps, mx_done, o_done = (
            [sem(f"{n}{m}") for m in "ab"] for n in ("cur_done", "ex_done", "lg_act", "lg_ps", "mx_done", "o_done"))
        o_evac, pT_act, pT_dve, pT_ps, p_done, v_used = (
            [sem(f"{n}{m}") for m in "ab"] for n in ("o_evac", "pT_act", "pT_dve", "pT_ps", "p_done", "v_used"))
        k_in = [[sem(f"k_in{m}{i}") for i in range(4)] for m in "ab"]
        v_in = [[sem(f"v_in{m}{i}") for i in range(2)] for m in "ab"]
        o_in = [sem(f"o_in{i}") for i in range(2)]
        kix_in = [sem(f"kix_in{i}") for i in range(4)]
        state_in = [sem(f"state_in{i}") for i in range(2)]
        state_out = [sem(f"state_out{i}") for i in range(2)]
        N_CONST, N_CIN, N_IIN = 5, 10, 5
        NPOOL = a["cache_a_k"].shape[1]

        def wv(name):
            return a[name][0].rearrange("(k p) n -> p k n", p=P)

        W = {n: wv(n) for n in ("w_in", "w_pa", "w_pb", "w_pc", "w_out", "ffn_up", "ffn_gate", "ffn_down")}
        X = {"h": (h_hi, h_lo), "o": (o_hi, o_lo), "m": (m_hi, m_lo), "y": (y_hi, y_lo)}

        def job(w, col, src, xk=0, k=KD, wk=0, ncol=COLS):
            step = KU if ncol == COLS else KD
            return [(W[w], wk + k0, min(step, k - k0), col, ncol, src, xk + k0) for k0 in range(0, k, step)]

        def jobs_in(c0):
            return lambda i: [job("w_in", c0 + (2 * i + j) * COLS, "h") for j in range(2)]

        def jobs_merge(i):
            return [job("w_in", C_GATE + i * COLS, "h"), job("w_pa", i * COLS, "o", O_A, 8),
                    job("w_in", C_GATE + D + i * COLS, "h"), job("w_pb", i * COLS, "o", O_B, 8),
                    job("w_in", C_GATE + 2 * D + i * COLS, "h"), job("w_pc", i * COLS, "o", O_C, 16)]

        def jobs_out(i):
            return [job("w_out", (2 * i + j) * COLS, "m") for j in range(2)]

        def jobs_ff(b0):
            return lambda i: [job("ffn_up", b0 * P + i * COLS, "h"), job("ffn_gate", b0 * P + i * COLS, "h")]

        def jobs_down(b0, k):
            return lambda i: [job("ffn_down", (2 * i + j) * COLS, "y", 0, k, b0) for j in range(2)]

        STAGES, at_u, at_j = {}, 0, 0
        for name, n, fn in (
                ("C", 12, jobs_in(C_QC)), ("A", 5, jobs_in(C_QA)),
                ("KI", 1, lambda i: [job("w_in", C_KI, "h", ncol=P)]),
                ("B", 3, jobs_in(C_QB)), ("M", 8, jobs_merge), ("O", 4, jobs_out),
                ("F1", KF1 // 2, jobs_ff(0)), ("D1", 4, jobs_down(0, KF1)),
                ("F2", KF2 // 2, jobs_ff(KF1)),
                ("F3", 1, lambda i: [job(w, (KF - 1) * P, "h", ncol=P) for w in ("ffn_up", "ffn_gate")]),
                ("D2", 4, jobs_down(KF1, KF2))):
            nu, nj = sum(len(j) for j in fn(0)), len(fn(0))
            STAGES[name] = (n, fn, at_u, at_j, nu, nj)
            assert n == 1 or (nu % 2 == 0 and nj % 2 == 0)
            at_u, at_j = at_u + n * nu, at_j + n * nj

        O_GROUPS, c, g0 = {}, 0, 0
        for (_, _, nk, _, _, src, xk) in (x for j in jobs_merge(0) for x in j):
            if src == "o":
                O_GROUPS[c] = range(g0, (xk + nk) // 4)
                g0 = (xk + nk) // 4
            c += 1

        def slot_of(w, slot, nk, ncol):
            return w[:, slot, 0:nk * ncol].rearrange("p (k n) -> p k n", k=nk)

        def sp_stage(sp, name):
            n, fn, u0, j0, nu, nj = STAGES[name]

            def body(i):
                for c, (w, k0, nk, col, ncol, _, _) in enumerate(x for j in fn(i) for x in j):
                    s = (u0 + c) % 2
                    if u0 + c >= 2 or not isinstance(i, int):
                        wait_apart(sp, w_split, u0 + i * nu + c - 1)
                    sp.dma_start(slot_of(w_raw, s, nk, ncol), w[:, k0:k0 + nk, bass.ds(col, ncol)])\
                        .then_inc(w_arrived[s], 16)

            first = 1 if u0 < 2 else 0
            if first or n == 1:
                body(0)
            if n > 1:
                with sp.Fori(first, n) as i:
                    body(i)

        def lagged(eng, chain, name, unit, evac, per, before):
            n, fn, u0, j0, nu, nj = STAGES[name]

            def body(i, first):
                c = 0
                for j, units in enumerate(fn(i)):
                    for (w, k0, nk, col, ncol, _, _) in units:
                        if before and isinstance(i, int):
                            before(c)
                        unit(u0 + i * nu + c, (u0 + c) % 2, nk * ncol, (u0 + c) // 2 + i * (nu // 2))
                        c += 1
                    if j or not first:
                        prev, ii = (j - 1, i) if j else (nj - 1, i - 1)
                        used = u0 + i * nu + c - len(units)
                        evac(prev, ii, (j0 + prev) % 2, used)
            body(0, True)
            if n > 1:
                with chain.loop(1, n, per) as i:
                    body(i, False)
            evac(nj - 1, n - 1, (j0 + nj - 1) % 2, u0 + n * nu)

        def act_stage(act, chain, name, evac, per=0, before=None):
            def unit(u, s, size, in_slot):
                act.wait_ge(w_arrived[s], 16 * (in_slot + 1))
                if not isinstance(u, int) or u >= 2:
                    act.wait_ge(w_used, u - 1)
                nc.scalar.activation(w_hi[:, s, 0:size], w_raw[:, s, 0:size], ACT.Copy).then_inc(w_hi_done, 1)
            lagged(act, chain, name, unit, evac, per, before)

        def dve_stage(dve, chain, name, evac, per=0, before=None):
            def unit(u, s, size, in_slot):
                dve.wait_ge(w_hi_done, u + 1)
                nc.vector.tensor_tensor(w_lo[:, s, 0:size], w_raw[:, s, 0:size],
                                        w_hi[:, s, 0:size].bitcast(F32), ALU.subtract).then_inc(w_split, 1)
            lagged(dve, chain, name, unit, evac, per, before)

        def pe_stage(pe, name):
            n, fn, u0, j0, nu, nj = STAGES[name]

            def body(i):
                c = 0
                for j, units in enumerate(fn(i)):
                    q = (j0 + j) % 2
                    if j0 + j >= 2 or not isinstance(i, int):
                        pe.wait_ge(bank_free[q], (j0 + j) // 2 + i * (nj // 2))
                    for m, (w, k0, nk, col, ncol, src, xk) in enumerate(units):
                        s = (u0 + c) % 2
                        xh, xl = X[src]
                        pe.wait_ge(w_split, u0 + i * nu + c + 1)
                        if src == "o":
                            pe.wait_ge(o_split, (xk + nk) // 4)
                        hi, lo = slot_of(w_hi, s, nk, ncol), slot_of(w_lo, s, nk, ncol)
                        for k in range(nk):
                            for b in range(ncol // P):
                                for t, (wp, xp) in enumerate(((hi, xh), (hi, xl), (lo, xh))):
                                    mm = nc.tensor.matmul(
                                        dense[:, 2 * q + b, 0:T], wp[:, k, b * P:(b + 1) * P], xp[:, xk + k, :],
                                        start=(m == 0 and k == 0 and t == 0),
                                        stop=(m == len(units) - 1 and k == nk - 1 and t == 2))
                        mm.then_inc(w_used, 1)
                        c += 1
            if n == 1:
                body(0)
            elif j0 < 2:
                body(0)
                with pe.Fori(1, n) as i:
                    body(i)
            else:
                with pe.Fori(0, n) as i:
                    body(i)

        block = ctx.enter_context(nc.Block())

        def pages_index(eng, c, half):
            for b in range(half, NB, 2):
                if not isinstance(c, int) or b >= 4:
                    wait_apart(eng, kxT_used, c * NB + b - 3)
                for j in range(4):
                    page = eng.value_load(pt_sb[0:1, bass.ds(c * 4 + (b * NPG + j), 1)],
                                          min_val=0, max_val=NPOOL - 1)
                    eng.dma_start(kixT[:, b % 4, j, :], a["cache_a_kidx"][0][bass.ds(page, 1), :, :]
                                  .rearrange("a p d -> (a p) d")).then_inc(kix_in[b % 4], 16)

        def pages(eng, b, cache, dst, lots, sems, free):
            for p in range(NPG):
                if p % (NPG // lots) == 0 and (not isinstance(b, int) or b > 0):
                    free(p // (NPG // lots))
                page = eng.value_load(pt_sb[0:1, bass.ds(b * NPG + p, 1)], min_val=0, max_val=NPOOL - 1)
                src = a[cache][0][bass.ds(page, 1)]
                src = src.rearrange("a p g d -> (a p) g d") if dst is kpg else src.rearrange("a p g d -> (a p) (g d)")
                eng.dma_start(dst[:, p], src).then_inc(sems[p // (NPG // lots)], 16)

        @block.sync
        def _(sp):
            def pages_k(mx, b):
                pages(sp, b, ("cache_a_k", "cache_b_k")[mx], kpg, 4, k_in[mx],
                      lambda lot: wait_apart(sp, lg_ps[mx], 5 * b + lot - 4))

            sp_stage(sp, "C")
            sp_stage(sp, "A")
            sp_stage(sp, "KI")
            sp.wait_ge(consts_in, 16 * N_CONST)
            sp.wait_ge(phase_act, 3)
            sp.wait_ge(phase_dve, 3)
            sp.wait_ge(phase_pool, 3)
            pages_index(sp, 0, 0)
            with sp.Fori(1, NPG // 4) as c:
                pages_index(sp, c, 0)
            for mx, ph in ((0, 6), (1, 9)):
                sp.wait_ge(phase_act, ph)
                sp.wait_ge(phase_dve, ph)
                pages_k(mx, 0)
                with sp.Fori(1, NB) as b:
                    pages_k(mx, b)
                if mx == 0:
                    sp_stage(sp, "B")
            for s in ("M", "O", "F1", "D1", "F2", "F3", "D2"):
                sp_stage(sp, s)

        @block.gpsimd
        def _(pool):
            def phase(k):
                pool.sem_inc(phase_pool, 1)
                pool.wait_ge(phase_act, k)
                pool.wait_ge(phase_dve, k)

            def load(dst, src, s):
                pool.dma_start(dst, src, allow_slow_non_contiguous=True).then_inc(s, 16)

            nst = [0]

            def store(dst, src):
                pool.dma_start(dst, src).then_inc(stored, 16)
                nst[0] += 1

            def stores_done():
                pool.wait_ge(stored, 16 * nst[0])

            load(ident[:, :], a["c_ident"], consts_in)
            for g, n in ((gmix, "norm_mix"), (gffn, "norm_ffn")):
                load(g[:, :], a[n], consts_in)
            load(gfin[:, :], a["norm_final"], consts_in)
            load(pt_sb[:, :], a["page_table"].rearrange("(o b) n -> o (b n)", o=1), consts_in)
            phase(1)
            for dst, n in ((rotJ, "c_rot"), (cosT, "c_cos"), (sinT, "c_sin"), (tailP, "c_tailp")):
                load(dst[:, :], a[n], c_in)
            for dst, n in ((intraP, "c_intrap"), (intraS, "c_intras"), (crossT, "c_cross"), (tailS, "c_tails"),
                           (decay, "c_decay")):
                load(dst[:, :, :], a[n], c_in)
            load(retgn[:, :], a["ret_gn"], c_in)

            def state_src(x, h):
                return x[0][:, bass.ds(h, 1), :, :].rearrange("b o d v -> d (b o) v")

            for s in range(2):
                load(state[:, s, :, :], state_src(a["state_ret"], s), state_in[s])
            phase(2)

            def head_out(i, more):
                for s in range(2):
                    h = 2 * i + s
                    pool.wait_ge(c_new, h + 1)
                    pool.dma_start(state_src(out["ret_s"], h), state[:, s, :, :]).then_inc(state_out[s], 16)
                    pool.dma_start(out["ret_p"][0, 0][bass.ds(h, 1), :, :].rearrange("o d v -> (o d) v"),
                                   s_fin[:, :]).then_inc(retp_out, 16)
                    if more:
                        pool.wait_ge(state_out[s], i * 16 + 16)
                        load(state[:, s, :, :], state_src(a["state_ret"], h + 2), state_in[s])
            with pool.Fori(0, H // 2 - 1) as i:
                head_out(i, True)
            head_out(H // 2 - 1, False)
            pool.wait_ge(state_out[0], 16 * H // 2)
            pool.wait_ge(state_out[1], 16 * H // 2)
            pool.wait_ge(retp_out, 16 * H)
            pool.wait_ge(c_head, H)
            store(o_scr[O_C:O_C + 16].rearrange("b p t -> p b t"), zc[:, 32:48, :])
            stores_done()
            phase(3)
            for dst, src in ((onehot[:, :], a["c_onehot"]), (tabx[0:NBUCK, :], a["rel_bias"]),
                             (causP[:, :, :], a["c_causp"]), (causS[:, :], a["c_causs"]),
                             (csel[:, :, :], a["c_sel"])):
                load(dst, src, i_in)
            phase(4)
            load(ki2[0:DI, :], za[0:DI, 20, :], ki_in)
            load(ki2[DI:P, :], za[0:DI, 20, :], ki_in)
            load(qodd[:, :, :], za[DI:P, 12:20, TP:T], ki_in)
            store(w_scr, wqb[DI:DI + HI, :])
            stores_done()
            load(wcol[:, :], w_scr.rearrange("h (q b) -> (h q) b", b=NB), ki_in)

            pages_index(pool, 0, 1)
            with pool.Fori(1, NPG // 4) as c:
                pages_index(pool, c, 1)
            pool.wait_ge(r_made, 1)
            store(r_scr, rvec[:, :])
            stores_done()
            for m in range(2):
                off = m * H * RVEC
                for q in range(TS):
                    load(near[q:NS:TS, m, :], bass.AP(r_scr.tensor, off + RD0 - PAGE - q, [[RVEC, H], [1, 136]]), near_in)
                load(far[:, m:m + 1], bass.AP(r_scr.tensor, off, [[RVEC, H], [0, TS], [1, 1]]), near_in)
            store(out["kv_a"], za[:, 8:12, :])
            store(out["ki"], za[0:DI, 20, :])
            stores_done()
            phase(5)

            def attention(mx):
                load(strip_rev[:, :, :], bass.AP(r_scr.tensor, mx * H * RVEC, [[1, P], [RVEC, H], [1, 384]]), strip_in)
                load(anti[:, :], a["c_anti"], strip_in)
                phase(6 + 3 * mx)
                if mx == 0:
                    load(eall[:, :, :], a["c_eall"], eall_in)

                def pages_v(b):
                    pages(pool, b, ("cache_a_v", "cache_b_v")[mx], vpg, 2, v_in[mx],
                          lambda lot: wait_apart(pool, v_used[mx], 2 * b + lot - 1))
                pages_v(0)
                with pool.Fori(1, NB) as b:
                    pages_v(b)
                pool.wait_ge(o_evac[mx], NB)
                base = (O_A, O_B)[mx]
                store(o_scr[base:base + H].rearrange("b p t -> p b t"), oT[:, :, :])
                stores_done()
                if mx == 0:
                    phase(7)

            attention(0)
            phase(8)
            store(out["kv_b"], za[:, 8:12, :])
            attention(1)
            phase(10)
            for g in range(8):
                if g >= 2:
                    pool.wait_ge(o_split, g - 1)
                load(o_stage[:, g % 2, :, :], o_scr[4 * g:4 * g + 4].rearrange("b p t -> p b t"), o_in[g % 2])
            phase(11)
            phase(12)
            phase(13)
            load(x1[:, :, :], a["x"], x1_in)
            phase(14)
            phase(15)
            load(cw[:, 0:3, :], a["conv_w"], cw_in)
            load(cw[:, 3, :], a["conv_b"], cw_in)
            load(cst[:, :, :], a["state_conv"], cw_in)
            phase(16)
            pool.wait_ge(cend_done, KF // 2 + 1)
            store(out["conv_end"], cend[:, :, :])
            stores_done()
            phase(17)
            phase(18)
            pool.wait_ge(n_f, 12)
            store(out["y"], tmp1[:, :, :])
            stores_done()

        @block.tensor
        def _(pe):
            mmul, turn = nc.tensor.matmul, nc.tensor.transpose

            def phase(k):
                pe.wait_ge(phase_act, k)
                pe.wait_ge(phase_dve, k)

            def sums(src, r):
                pe.wait_ge(n_sq, r + 1)
                for k in range(KD):
                    mm = mmul(bank[4][:, 0:T], ones[:, :], src[:, k, :], start=(k == 0), stop=(k == KD - 1))
                mm.then_inc(n_sum, 1)

            pe.wait_ge(eps_set, 1)
            sums(tmp0, 0)
            phase(1)
            pe_stage(pe, "C")
            phase(2)
            pe.wait_ge(consts_in, 16 * N_CONST)
            pe.wait_ge(c_in, 16 * N_CIN)

            def retention(i):
                for s in range(2):
                    h = 2 * i + s
                    pe.wait_ge(c_head, h)
                    pe.wait_ge(c_new, h)
                    mmul(bank[4][:, 0:T], rotJ[:, :], zc[:, bass.ds(h, 1), :].rearrange("p o t -> p (o t)"),
                         start=True, stop=True)
                    mmul(bank[5][:, 0:T], rotJ[:, :], zc[:, bass.ds(h + 8, 1), :].rearrange("p o t -> p (o t)"),
                         start=True, stop=True).then_inc(c_rot, 1)
                    pe.wait_ge(c_qk, h + 1)
                    pe.wait_ge(c_vcur, h + 1)
                    for c in range(2):
                        turn(bank[6][:, c * P:(c + 1) * P], kr[:, c * P:(c + 1) * P], ident[:, :])
                    turn(bank[6][0:NS, 256:384], kr[:, TP:T], ident[:, :])
                    for b in range(2):
                        for c in range(2):
                            turn(bank[4][:, c * 256 + b * P:c * 256 + (b + 1) * P], vcur[:, b, c * P:(c + 1) * P],
                                 ident[:, :])
                        mm = turn(bank[5][0:NS, b * P:(b + 1) * P], vcur[:, b, TP:T], ident[:, :])
                    mm.then_inc(c_turned, 1)
                    for c in range(2):
                        mmul(bank[7][:, c * P:(c + 1) * P], kr[:, c * P:(c + 1) * P], qr[:, c * P:(c + 1) * P],
                             start=True, stop=True)
                    mmul(bank[7][0:NS, 256:320], kr[:, TP:T], qr[:, TP:T], start=True, stop=True).then_inc(c_att, 1)
                    pe.wait_ge(c_kn, h + 1)
                    pe.wait_ge(c_vn, h + 1)
                    for c in range(2):
                        mm = mmul(bank[6][:, c * 256:(c + 1) * 256], knP[:, c, :], vnP[:, c, :], start=True, stop=True)
                    mm.then_inc(c_s, 1)
                    pe.wait_ge(c_mid, h + 1)
                    pe.wait_ge(state_in[s], i * 16 + 16)
                    for b in range(2):
                        o, cb = bank[4 + b], slice(b * P, (b + 1) * P)
                        mmul(o[:, 0:P], vnP[:, 0, cb], attP[:, 0, :], start=True, stop=True)
                        mmul(o[:, P:TP], vnP[:, 1, cb], attP[:, 1, :], start=True, stop=False)
                        mmul(o[:, P:TP], s_mid[:, cb], qx[:, P:TP], start=False, stop=True)
                        mmul(o[:, TP:T], vnS[:, cb], attS[:, :], start=True, stop=True)
                        for r in range(NB):
                            c = slice(TP + r * TS, TP + (r + 1) * TS)
                            mm = mmul(o[:, c], state[:, s, r, cb], qx[:, c], start=False, stop=True,
                                      skip_group_check=True)
                    mm.then_inc(c_o, 1)
                    for r in range(NB):
                        mm = mmul(bank[r // 2][:, (r % 2) * 256:(r % 2 + 1) * 256], kexp[0:NS, r, :], vnS[:, :],
                                  start=True, stop=True)
                    mm.then_inc(c_snew, 1)
                    pe.wait_ge(c_sq, h + 1)
                    pe.wait_ge(c_fin, h + 1)
                    for b in range(2):
                        mm = mmul(bank[6][:, 0:T], ones[:, :], vcur[:, b, :], start=(b == 0), stop=(b == 1))
                    mm.then_inc(c_ss, 1)

            with pe.Fori(0, H // 2) as i:
                retention(i)
            phase(3)

            pe_stage(pe, "A")
            pe_stage(pe, "KI")
            pe.wait_ge(i_in, 16 * N_IIN)
            pe.wait_ge(tabx_set, 1)
            mmul(bank[4][0:16, :], tabx[:, :], onehot[:, :], start=True, stop=True).then_inc(r_ps, 1)
            phase(4)

            def natural(mx):
                for t in range(2):
                    for j in range(2):
                        mm = turn(bank[4 + t][:, j * P:(j + 1) * P], za[:, 10 + j, t * P:(t + 1) * P], ident[:, :])
                    mm.then_inc(nat_ps, 1)

            natural(0)
            for t in range(2):
                mm = turn(bank[7][:, t * 80:(t + 1) * 80], za[0:80, 20, t * P:(t + 1) * P], ident[0:80, 0:80])
            mm.then_inc(kin_ps, 1)
            pe.wait_ge(ki_in, 64)
            n = 0
            for t in range(2):
                for hp in range(HI // 2):
                    if n >= 2:
                        pe.wait_ge(ix_relu, n - 1)
                    for o in range(2):
                        rows = slice(o * DI, (o + 1) * DI)
                        mm = mmul(bank[2 * (n % 2) + o][:, 0:TP], za[rows, 12 + hp, t * P:(t + 1) * P],
                                  ki2[rows, 0:TP], start=True, stop=True)
                        mm.then_inc(ix_s, 1)
                    n += 1
            pe.wait_ge(qi_ready, 1)
            pe.wait_ge(nat_done, 2)
            for b in range(NB):
                mm = mmul(bank[6][:, b * TS:(b + 1) * TS], qi64[:, b, :, :].rearrange("p h q -> p (h q)"),
                          ki2[0:DI, TP + b * TS:TP + (b + 1) * TS], start=True, stop=True)
            mm.then_inc(dn_s, 1)
            pe.wait_ge(dn_relu, 1)
            for b in range(NB):
                mm = mmul(bank[3][0:NS, 0:TS], wsel[:, b, :], rel[:, 0, b * TS:(b + 1) * TS],
                          start=(b == 0), stop=(b == NB - 1))
            mm.then_inc(dn_w, 1)

            def index_chunk(c):
                first = isinstance(c, int)
                for st in range(NB + 1):
                    if st < NB:
                        b = st
                        wait_apart(pe, kix_in[b % 4], c * 128 + (b // 4) * 64 + 64)
                        if not first or b >= 2:
                            pe.wait_ge(rel_done, c * NB + b - 1)
                        else:
                            pe.wait_ge(dn_w, 1)
                        mmul(bank[6 + b % 2][:, :], qi64[:, b, :, :].rearrange("p h q -> p (h q)"),
                             kixT[:, b % 4, :, :], start=True, stop=True).then_inc(kxT_used, 1)
                    if st >= 1:
                        b = st - 1
                        pe.wait_ge(rel_done, c * NB + b + 1)
                        if b == 0 and not first:
                            pe.wait_ge(sc_done, c)
                        mmul(bank[2][0:NS, :], wsel[:, b, :], rel[:, b % 2, :], start=(b == 0), stop=(b == NB - 1))\
                            .then_inc(rel_used, 1)
            index_chunk(0)
            with pe.Fori(1, NPG // 4) as c:
                index_chunk(c)
            phase(5)

            def attention(mx):
                N = 2 * H
                pe.wait_ge(strip_in, 32 * (mx + 1))
                for h in range(H):
                    if h >= 4:
                        pe.wait_ge(strip_evac, mx * H + h - 3)
                    mmul(bank[h % 4][:, 0:384], anti[:, :], strip_rev[:, h, :], start=True, stop=True)\
                        .then_inc(strip_ps, 1)
                pe.wait_ge(strip_evac, mx * H + H)
                pe.wait_ge(nat_done, 2 * mx + 2)
                for n in range(N + 1):
                    if n < N:
                        t, h = n // H, n % H
                        nk = (t + 1) * P
                        if n >= 2:
                            pe.wait_ge(pl_evac, mx * 2 * H + n - 1)
                        mm = mmul(bank[n % 2][:, 0:nk], za[:, h, t * P:(t + 1) * P], za[:, 8 + h // GRP, 0:nk],
                                  start=True, stop=(mx == 1))
                        if mx == 0:
                            mm = mmul(bank[n % 2][:, 0:nk], identb[:, :], sel16[:, t, 0:nk], start=False, stop=True)
                        mm.then_inc(pl_done, 1)
                    if n >= 1:
                        m = n - 1
                        t, h = m // H, m % H
                        pe.wait_ge(pp_done, mx * 2 * H + m + 1)
                        for kt in range(t + 1):
                            mm = turn(bank[4 + m % 2][:, kt * P:(kt + 1) * P], lgP[:, m % 2, kt * P:(kt + 1) * P],
                                      ident[:, :])
                        mm.then_inc(pt_ps, 1)
                        pe.wait_ge(pt_evac, mx * 2 * H + m + 1)
                        if m >= 2:
                            pe.wait_ge(po_evac, mx * 2 * H + m - 1)
                        g = h // GRP
                        for kt in range(t + 1):
                            mm = mmul(bank[6 + m % 2][:, 0:P], vnat[:, kt, g * P:(g + 1) * P],
                                      pTP[:, m % 2, kt * P:(kt + 1) * P], start=(kt == 0), stop=(kt == t))
                        mm.then_inc(po_done, 1)
                phase(6 + 3 * mx)

                def logits(b, s):
                    pe.wait_ge(cur_done[mx], b + 1)
                    if mx == 0:
                        pe.wait_ge(ecur_done, b + 1)
                    for c in range(4):
                        if not isinstance(b, int) or b > 0:
                            if c < 3:
                                pe.wait_ge(lg_act[mx], 3 * b + c - 2)
                            else:
                                pe.wait_ge(mx_done[mx], b)
                        pe.wait_ge(k_in[mx][c], b * 64 + 64)
                        for g in range(2):
                            mm = mmul(bank[c][g * 32:(g + 1) * 32, :],
                                      qcur[:, s, g * GRP:(g + 1) * GRP, :].rearrange("p r q -> p (r q)"),
                                      kpg[:, 4 * c:4 * c + 4, g, :], start=True, stop=True)
                        if mx == 0:
                            mm = mmul(bank[c][0:NS, :], ecur[:, s, :], m16[:, c * 512:(c + 1) * 512],
                                      start=False, stop=True, skip_group_check=True)
                        mm.then_inc(lg_ps[mx], 1)
                    for g in range(2):
                        mmul(bank[6][g * 32:(g + 1) * 32, 0:TS],
                             qcur[:, s, g * GRP:(g + 1) * GRP, :].rearrange("p r q -> p (r q)"),
                             kvcur[:, s, g, :], start=True, stop=True)
                    if mx == 0:
                        mmul(bank[6][0:NS, 0:TS], ecur[:, s, :], m16[:, PAST:L], start=False, stop=True,
                             skip_group_check=True)
                    for g in range(2):
                        mm = turn(bank[6][0:TS, P + g * P:P + (g + 1) * P], kvcur[:, s, 2 + g, :], ident[:, :])
                    mm.then_inc(lg_ps[mx], 1)

                def output(b, s):
                    wait_apart(pe, p_done[mx], b + 1)
                    for half in range(2):
                        for p in range(8 * half, 8 * half + 8):
                            mm = turn(bank[4 + half][:, (p % 8) * NS:(p % 8 + 1) * NS], lg[:, s, p * P:(p + 1) * P],
                                      ident[0:NS, 0:NS])
                        if half == 0:
                            mm.then_inc(pT_ps[mx], 1)
                    if not isinstance(b, int) or b > 0:
                        wait_apart(pe, o_evac[mx], b)
                    turn(bank[7][0:TS, NS:2 * NS], lg[:, s, PAST:L], ident[0:NS, 0:NS]).then_inc(pT_ps[mx], 1)
                    pe.wait_ge(pT_act[mx], b + 1)
                    pe.wait_ge(pT_dve[mx], b + 1)
                    for p in range(NPG):
                        if p % 8 == 0:
                            pe.wait_ge(v_in[mx][p // 8], b * 128 + 128)
                        for g in range(2):
                            cols = slice(g * 32, (g + 1) * 32)
                            mm = mmul(bank[7][:, cols], vpg[:, p, g * P:(g + 1) * P], pT[:, p, cols],
                                      start=(p == 0 and g == 0), stop=False, skip_group_check=True)
                        if p % 8 == 7:
                            mm.then_inc(v_used[mx], 1)
                    for g in range(2):
                        cols = slice(g * 32, (g + 1) * 32)
                        mm = mmul(bank[7][:, cols], vnew[:, s, g * P:(g + 1) * P], pTn[:, cols], start=False,
                                  stop=True, skip_group_check=True)
                    mm.then_inc(o_done[mx], 1)

                logits(0, 0)
                logits(1, 1)
                output(0, 0)
                with pe.Fori(0, NB // 2 - 1) as i:
                    logits(2 * i + 2, 0)
                    output(2 * i + 1, 1)
                    logits(2 * i + 3, 1)
                    output(2 * i + 2, 0)
                output(NB - 1, 1)
                phase(7 + 3 * mx)

            attention(0)
            pe_stage(pe, "B")
            phase(8)
            natural(1)
            attention(1)
            pe_stage(pe, "M")
            phase(13)
            pe_stage(pe, "O")
            phase(14)
            sums(tmp1, 1)
            phase(15)

            pe_stage(pe, "F1")
            phase(16)
            pe_stage(pe, "D1")
            pe_stage(pe, "F2")
            pe_stage(pe, "F3")
            phase(17)
            pe_stage(pe, "D2")
            phase(18)
            sums(tmp1, 2)

        def evacuated(eng, name):
            n, fn, u0, j0, nu, nj = STAGES[name]
            done = j0 + n * nj
            eng.wait_ge(bank_free[0], (done + 1) // 2)
            if done > 1:
                eng.wait_ge(bank_free[1], done // 2)

        @block.scalar
        def _(act):
            A = Chain(act, act_chain)
            fn = nc.scalar.activation

            def phase(k, pool=True):
                act.sem_inc(phase_act, 1)
                act.wait_ge(phase_dve, k)
                if pool:
                    act.wait_ge(phase_pool, k)

            def norm(src, tmp, r, split):
                fn(tmp[:, :, :], src[:, :, :], ACT.Square).then_inc(n_sq, 1)
                act.wait_ge(n_sum, r + 1)
                fn(rstd[:, :], bank[4][:, 0:T], ACT.Sqrt, bias=epsc[:, :], scale=1.0 / D).then_inc(n_root, 1)
                if split:
                    for g in range(4):
                        act.wait_ge(n_f, 4 * r + g + 1)
                        ks = slice(4 * g, 4 * g + 4)
                        fn(h_hi[:, ks, :], tmp[:, ks, :], ACT.Copy).then_inc(n_hi, 1)

            for g in range(2):
                ks = slice(8 * g, 8 * g + 8)
                act.dma_start(xT0[:, ks, :], a["x"][:, ks, :]).then_inc(x_arrived, 16)
            act.wait_ge(x_arrived, 32)
            act.wait_ge(eps_set, 1)
            norm(xT0, tmp0, 0, True)
            act.wait_ge(n_hi, 4)
            phase(1)

            def to_blocks(dst):
                def evac(j, i, q, used):
                    if dst is za:
                        act.wait_ge(phase_pool, 3)
                    act.wait_ge(w_used, used)
                    fn(dst[:, bass.ds(4 * i + 2 * j, 2), :], dense[:, 2 * q:2 * q + 2, 0:T], ACT.Copy)\
                        .then_inc(bank_free[q], 1)
                return evac

            act_stage(act, A, "C", to_blocks(zc))
            evacuated(act, "C")
            phase(2)

            def retention(i):
                for s in range(2):
                    h = 2 * i + s
                    act.wait_ge(c_head, h)
                    act.wait_ge(c_new, h)
                    fn(vcur[:, :, :], zc[:, bass.ds(2 * h + 16, 2), :], ACT.Copy).then_inc(c_vcur, 1)
                    fn(silu[:, :, :], zc[:, bass.ds(2 * h + 32, 2), :], ACT.Silu).then_inc(c_silu, 1)
                    act.wait_ge(c_turned, h + 1)
                    fn(vnP[:, :, :].rearrange("p c v -> p (c v)"), bank[4], ACT.Copy)
                    fn(vnS[:, :], bank[5][0:NS, 0:256], ACT.Copy).then_inc(c_vn, 1)
                    act.wait_ge(c_s, h + 1)
                    fn(s_mid[:, :], bank[6][:, 0:256], ACT.Copy).then_inc(c_mid, 1)
                    act.wait_ge(c_o, h + 1)
                    for b in range(2):
                        ins = fn(vcur[:, b, :], bank[4 + b][:, 0:T], ACT.Square)
                    ins.then_inc(c_sq, 1)
                    act.wait_ge(c_ss, h + 1)
                    fn(rstd[:, :], bank[6][:, 0:T], ACT.Sqrt, bias=epsc[:, :], scale=1.0 / 256).then_inc(c_root, 1)
            with act.Fori(0, H // 2) as i:
                retention(i)
            phase(3, False)
            act_stage(act, A, "A", to_blocks(za))

            def ki_block(j, i, q, used):
                act.wait_ge(w_used, used)
                fn(za[:, 20, :], dense[:, 2 * q, 0:T], ACT.Copy).then_inc(bank_free[q], 1)
            act_stage(act, A, "KI", ki_block)
            evacuated(act, "KI")
            act.wait_ge(r_ps, 1)
            fn(rvec[:, :], bank[4][0:16, :], ACT.Copy).then_inc(r_made, 1)
            act.wait_ge(r_made, 1)
            A(fn(wqb[DI:DI + HI, :].rearrange("h (q b) -> h q b", b=NB),
                 za[DI:DI + HI, 20, TP:T].rearrange("h (b q) -> h q b", q=TS), ACT.Copy))
            phase(4)

            def scale_and_natural(mx):
                A(fn(za[:, 0:H, :], za[:, 0:H, :], ACT.Copy, scale=SCALE))
                for t in range(2):
                    act.wait_ge(nat_ps, 2 * mx + t + 1)
                    fn(vnat[:, t, :], bank[4 + t][:, 0:256], ACT.Copy).then_inc(nat_done, 1)
                act.wait_ge(nat_done, 2 * mx + 2)

            scale_and_natural(0)
            act.wait_ge(kin_ps, 1)
            for t in range(2):
                fn(kin[:, t, :], bank[7][:, t * 80:(t + 1) * 80], ACT.Copy).then_inc(kin_done, 1)
            A(fn(identb[:, :], ident[:, :], ACT.Copy))
            rs = (DI * HI) ** -0.5
            for n in range(HI):
                act.wait_ge(ix_s, 2 * n + 2)
                if n >= 2:
                    act.wait_ge(ix_used, n - 1)
                fn(rel[:, n % 2, :].rearrange("p (o k) -> p o k", o=2),
                   dense[:, 2 * (n % 2):2 * (n % 2) + 2, 0:TP], ACT.Relu, scale=rs).then_inc(ix_relu, 1)
            act.wait_ge(ix_used, HI)
            act.wait_ge(dn_s, 1)
            fn(rel[:, 0, 0:NS], bank[6][:, 0:NS], ACT.Relu, scale=rs).then_inc(dn_relu, 1)
            act.wait_ge(dn_w, 1)

            def index_chunk(c):
                for b in range(NB):
                    act.wait_ge(kxT_used, c * NB + b + 1)
                    if not isinstance(c, int) or b >= 2:
                        act.wait_ge(rel_used, c * NB + b - 1)
                    fn(rel[:, b % 2, :], bank[6 + b % 2], ACT.Relu, scale=rs).then_inc(rel_done, 1)
            index_chunk(0)
            with act.Fori(1, NPG // 4) as c:
                index_chunk(c)
            phase(5)

            def attention(mx):
                N = 2 * H
                for n in range(N + 2):
                    if n < N:
                        nk = (n // H + 1) * P
                        act.wait_ge(pm_done, mx * 2 * H + n + 1)
                        fn(lgP[:, n % 2, 0:nk], lgP[:, n % 2, 0:nk], ACT.Exp, bias=stP[:, n % 2, 1:2],
                           accum_out=stP[:, n % 2, 2:3]).then_inc(px_done, 1)
                    if 1 <= n <= N:
                        m = n - 1
                        nk = (m // H + 1) * P
                        act.wait_ge(pt_ps, mx * 2 * H + m + 1)
                        if m >= 2:
                            act.wait_ge(po_done, mx * 2 * H + m - 1)
                        fn(pTP[:, m % 2, 0:nk], bank[4 + m % 2][:, 0:nk], ACT.Copy).then_inc(pt_evac, 1)
                    if n >= 2:
                        m = n - 2
                        t, h = m // H, m % H
                        act.wait_ge(po_done, mx * 2 * H + m + 1)
                        fn(oT[:, h, t * P:(t + 1) * P], bank[6 + m % 2][:, 0:P], ACT.Copy).then_inc(po_evac, 1)
                act.wait_ge(po_evac, mx * 2 * H + N)
                phase(6 + 3 * mx)

                def cur(b, s):
                    cols = bass.ds(b * TS + TP, TS)
                    fn(qcur[:, s, :, :], za[:, 0:H, cols], ACT.Copy)
                    fn(kvcur[:, s, :, :], za[:, H:H + 4, cols], ACT.Copy).then_inc(cur_done[mx], 1)

                def logits(b, s):
                    for c in range(3):
                        act.wait_ge(lg_ps[mx], 5 * b + c + 1)
                        if mx == 1:
                            act.wait_ge(gate_done, b * 4 + c + 1)
                        fn(lg[:, s, c * 512:(c + 1) * 512], bank[c][0:NS, :], ACT.Identity, bias=far[:, mx:mx + 1])\
                            .then_inc(lg_act[mx], 1)

                def exps(b, s):
                    act.wait_ge(mx_done[mx], b + 1)
                    fn(lg[:, s, :], lg[:, s, :], ACT.Exp, bias=stS[:, s, 1:2], accum_out=stS[:, s, 2:3])\
                        .then_inc(ex_done[mx], 1)

                def output(b):
                    act.wait_ge(pT_ps[mx], 2 * b + 1)
                    fn(pT[:, 0:8, :].rearrange("p k q -> p (k q)"), bank[4], ACT.Copy).then_inc(pT_act[mx], 1)
                    act.wait_ge(o_done[mx], b + 1)
                    fn(oT[:, :, bass.ds(b * TS + TP, TS)], bank[7][:, 0:NS].rearrange("p (h q) -> p h q", q=TS),
                       ACT.Copy).then_inc(o_evac[mx], 1)

                def step(b, s, more=True):
                    exps(b, s)
                    logits(b + 1, 1 - s)
                    if more:
                        cur(b + 2, s)
                    output(b)
                act.wait_ge(near_in, 16 * 2 * (TS + 1))
                cur(0, 0)
                cur(1, 1)
                logits(0, 0)
                step(0, 0)
                with act.Fori(0, NB // 2 - 2) as i:
                    step(2 * i + 1, 1)
                    step(2 * i + 2, 0)
                step(NB - 3, 1)
                step(NB - 2, 0, False)
                exps(NB - 1, 1)
                output(NB - 1)
                act.wait_ge(o_evac[mx], NB)
                phase(7 + 3 * mx, mx == 0)

            attention(0)
            act_stage(act, A, "B", to_blocks(za))
            evacuated(act, "B")
            phase(8)
            scale_and_natural(1)
            attention(1)

            def split_o(c):
                for g in O_GROUPS.get(c, ()):
                    act.wait_ge(o_in[g % 2], 16 * (g // 2 + 1))
                    fn(o_hi[:, 4 * g:4 * g + 4, :], o_stage[:, g % 2, :, :], ACT.Copy).then_inc(o_hi_done, 1)
            mj0 = STAGES["M"][3]

            def gates(j, i, q, used):
                if j % 2 == 0:
                    act.wait_ge(w_used, used)
                    act.wait_ge(bank_free[1 - q], (mj0 + j - 1) // 2 + 3 * i + 1)
                    fn(sig[:, :, :], dense[:, 2 * q:2 * q + 2, 0:T], ACT.Sigmoid).then_inc(bank_free[q], 1)
            act_stage(act, A, "M", gates, before=split_o)
            evacuated(act, "M")
            phase(11)
            phase(12)
            fn(m_hi[:, :, :], m_f[:, :, :], ACT.Copy).then_inc(m_hi_done, 1)
            act.wait_ge(m_hi_done, 1)
            phase(13)
            act_stage(act, A, "O", lambda j, i, q, used: None)
            phase(14)
            norm(x1, tmp1, 1, True)
            act.wait_ge(n_hi, 8)
            phase(15)

            def ff(base, yb, nb):
                def evac(j, i, q, used):
                    n = base + i
                    if j == 0:
                        act.wait_ge(w_used, used)
                        act.wait_ge(cv_made, n)
                        fn(ue[:, 0:nb, 2:2 + TP], dense[:, 2 * q:2 * q + nb, 0:TP], ACT.Copy)
                        for b in range(nb):
                            ins = fn(ue[:, b, 258:338].rearrange("p (r t) -> p r t", t=10)[:, :, 2:10],
                                     dense[:, 2 * q + b, TP:T].rearrange("p (r t) -> p r t", t=TS), ACT.Copy)
                        ins.then_inc(bank_free[q], 1)
                        for b in range(nb):
                            ins = fn(ue[:, b, 258:338].rearrange("p (r t) -> p r t", t=10)[:, :, 0:2],
                                     cst[:, bass.ds(2 * n + b, 1), :].rearrange("p o (r t) -> p (o r) t", t=2), ACT.Copy)
                        ins.then_inc(ue_done, 1)
                        act.wait_ge(ue_done, n + 1)
                        f2 = bass.ds(2 * n, nb)
                        fn(cend[:, f2, 0:2], ue[:, 0:nb, 256:258], ACT.Copy)
                        for b in range(nb):
                            ins = fn(cend[:, bass.ds(2 * n + b, 1), 2:18].rearrange("p o (r t) -> p (o r) t", t=2),
                                     ue[:, b, 258:338].rearrange("p (r t) -> p r t", t=10)[:, :, 8:10], ACT.Copy)
                        ins.then_inc(cend_done, 1)
                    else:
                        act.wait_ge(cv_made, n + 1)
                        act.wait_ge(y_done, n)
                        fn(yv[:, 0:nb, :], cv[:, 0:nb, :], ACT.Gelu).then_inc(g_done, 1)
                        act.wait_ge(ym_done, n + 1)
                        fn(y_hi[:, bass.ds(yb + 2 * i, nb), :], yv[:, 0:nb, :], ACT.Copy).then_inc(yh_done, 1)
                return evac
            act.wait_ge(cw_in, 48)
            act_stage(act, A, "F1", ff(0, 0, 2))
            act.wait_ge(yh_done, KF1 // 2)
            phase(16)
            act_stage(act, A, "D1", lambda j, i, q, used: None)
            act_stage(act, A, "F2", ff(KF1 // 2, 0, 2))
            act_stage(act, A, "F3", ff(KF // 2, KF2 - 1, 1))
            act.wait_ge(yh_done, KF // 2 + 1)
            phase(17)
            act_stage(act, A, "D2", lambda j, i, q, used: None)
            phase(18)
            norm(x1, tmp1, 2, False)

        @block.vector
        def _(dve):
            V = Chain(dve, dve_chain)
            tt, stt, ts = nc.vector.tensor_tensor, nc.vector.scalar_tensor_tensor, nc.vector.tensor_scalar
            copy = nc.vector.tensor_copy

            def phase(k, pool=True):
                dve.sem_inc(phase_dve, 1)
                dve.wait_ge(phase_act, k)
                if pool:
                    dve.wait_ge(phase_pool, k)

            def norm(src, tmp, g, r, split):
                dve.wait_ge(n_root, r + 1)
                V(nc.vector.reciprocal(rstd[:, :], rstd[:, :]))
                for k in range(KD):
                    ins = stt(tmp[:, k, :], src[:, k, :], g[:, k:k + 1], rstd[:, :], ALU.mult, ALU.mult)
                    if k % 4 == 3:
                        ins.then_inc(n_f, 1)
                dve.wait_ge(n_f, 4 * r + 4)
                if split:
                    for q in range(4):
                        dve.wait_ge(n_hi, 4 * r + q + 1)
                        ks = slice(4 * q, 4 * q + 4)
                        V(tt(h_lo[:, ks, :], tmp[:, ks, :], h_hi[:, ks, :].bitcast(F32), ALU.subtract))

            nc.vector.memset(epsc[:, :], EPS)
            nc.vector.memset(ones[:, :], 1.0).then_inc(eps_set, 1)
            dve.wait_ge(consts_in, 16 * N_CONST)
            norm(xT0, tmp0, gmix, 0, True)
            phase(1)

            def nothing(j, i, q, used):
                pass
            dve_stage(dve, V, "C", nothing)
            phase(2)
            dve.wait_ge(c_in, 16 * N_CIN)

            def retention(i):
                for s in range(2):
                    h = 2 * i + s

                    def blk(x, n=1):
                        v = zc[:, bass.ds(x, n), :]
                        return v.rearrange("p o t -> p (o t)") if n == 1 else v
                    dve.wait_ge(c_rot, h + 1)
                    V(tt(qr[:, :], blk(h), cosT[:, :], ALU.mult))
                    V(tt(qx[:, :], bank[4][:, 0:T], sinT[:, :], ALU.mult))
                    V(tt(qr[:, :], qr[:, :], qx[:, :], ALU.add))
                    V(stt(kr[:, :], blk(h + 8), SCALE, cosT[:, :], ALU.mult, ALU.mult))
                    V(stt(qx[:, :], bank[5][:, 0:T], SCALE, sinT[:, :], ALU.mult, ALU.mult))
                    ins = tt(kr[:, :], kr[:, :], qx[:, :], ALU.add)
                    ins.then_inc(c_qk, 1)
                    dve.wait_ge(c_qk, h + 1)
                    cr = crossT[:, bass.ds(h, 1), :].rearrange("p o t -> p (o t)")
                    V(tt(qx[:, P:TP], qr[:, P:TP], cr, ALU.mult))
                    V(tt(qx[:, TP:T].rearrange("p (r t) -> p r t", t=TS), qr[:, TP:T].rearrange("p (r t) -> p r t", t=TS),
                         cr[:, 0:TS].unsqueeze(1).to_broadcast([P, NB, TS]), ALU.mult))
                    dve.wait_ge(c_turned, h + 1)
                    V(ts(knP[:, :, :].rearrange("p c d -> p (c d)"), bank[6][:, 0:256], tailP[:, bass.ds(h, 1)], None,
                         ALU.mult))
                    V(tt(kexp[0:NS, :, :], bank[6][0:NS, 256:384].unsqueeze(1).to_broadcast([NS, NB, P]),
                         tailS[:, bass.ds(h, 1), :].rearrange("p o r -> p (o r)").unsqueeze(2).to_broadcast([NS, NB, P]),
                         ALU.mult))
                    dve.wait_ge(c_att, h + 1)
                    V(tt(attP[:, :, :], bank[7][:, 0:256].rearrange("p (c q) -> p c q", c=2),
                         intraP[:, bass.ds(h, 1), :].to_broadcast([P, 2, P]), ALU.mult))
                    ins = tt(attS[:, :], bank[7][0:NS, 256:320],
                             intraS[:, bass.ds(h, 1), :].rearrange("p o q -> p (o q)"), ALU.mult)
                    ins.then_inc(c_kn, 1)
                    dve.wait_ge(c_mid, h + 1)
                    dve.wait_ge(retp_out, h * 16)
                    stt(s_fin[:, :], s_mid[:, :], decay[:, 0, bass.ds(h, 1)], bank[6][:, 256:512],
                        ALU.mult, ALU.add).then_inc(c_fin, 1)
                    dve.wait_ge(c_fin, h + 1)
                    dve.wait_ge(c_snew, h + 1)
                    st_h = state[:, s, :, :].rearrange("p r v -> p (r v)")
                    stt(st_h, st_h, decay[:, 1, bass.ds(h, 1)], dense[:, :, :].rearrange("p b v -> p (b v)"),
                        ALU.mult, ALU.add).then_inc(c_new, 1)
                    dve.wait_ge(c_root, h + 1)
                    V(nc.vector.reciprocal(rstd[:, :], rstd[:, :]))
                    dve.wait_ge(c_silu, h + 1)
                    for b in range(2):
                        V(stt(blk(2 * h + 32 + b), bank[4 + b][:, 0:T], retgn[:, bass.ds(2 * h + b, 1)], rstd[:, :],
                              ALU.mult, ALU.mult))
                    tt(blk(2 * h + 32, 2), blk(2 * h + 32, 2), silu[:, :, :], ALU.mult).then_inc(c_head, 1)
                    dve.wait_ge(c_head, h + 1)
            with V.loop(0, H // 2, 2 * 13) as i:
                retention(i)
            dve.wait_ge(c_new, H)
            phase(3, False)
            dve_stage(dve, V, "A", nothing)
            dve_stage(dve, V, "KI", nothing)
            dve.wait_ge(phase_pool, 3)
            nc.vector.memset(tabx[NBUCK:NBUCK + 1, :], NEG).then_inc(tabx_set, 1)
            dve.wait_ge(tabx_set, 1)
            phase(4)
            dve.wait_ge(ki_in, 64)
            q_src = za[0:DI, 12:20, TP:T].rearrange("p j (b q) -> p b j q", q=TS)
            V(tt(wsel[:, :, :], csel[:, :, :], wcol[:, :].unsqueeze(2).to_broadcast([P, NB, NS]), ALU.mult))
            for b in range(NB):
                cs = slice(b * TS, (b + 1) * TS)
                V(copy(qi64[:, b, 0:HI:2, :], za[0:DI, 12:20, TP + b * TS:TP + (b + 1) * TS]))
                V(copy(qi64[:, b, 1:HI:2, :], qodd[:, :, cs]))
            dve.sem_inc(qi_ready, 1)
            dve.wait_ge(kin_done, 2)

            def take8(vals, rows, best):
                V(nc.vector.max(best[0:rows, :], vals), wait_apart)
                V(nc.vector.match_replace(vals, best[0:rows, :], vals, TAKEN), wait_apart)

            n = 0
            for t in range(2):
                for hp in range(HI // 2):
                    dve.wait_ge(ix_relu, n + 1)
                    for o in range(2):
                        h = 2 * hp + o
                        ins = stt(accP[:, :], rel[:, n % 2, o * TP:(o + 1) * TP], kin[:, t, DI + h:DI + h + 1],
                                  causP[:, t, :] if h == 0 else accP[:, :], ALU.mult, ALU.add)
                        if o == 0:
                            V(ins)
                    n += 1
                    ins.then_inc(ix_used, 1)
                    dve.wait_ge(ix_used, n)
                with V.loop(0, TP // 4 // 8, 2):
                    take8(accP[:, :], P, top8)
                V(ts(sel16[:, t, :], accP[:, :], TAKEN, NEG, ALU.not_equal, ALU.mult))
            dve.wait_ge(dn_w, 1)
            V(tt(score[:, PAST:L], bank[3][0:NS, 0:TS], causS[:, :], ALU.add))
            with dve.Fori(0, NPG // 4) as c:
                dve.wait_ge(rel_used, c * NB + NB)
                copy(score[:, bass.ds(c * 512, 512)], bank[2][0:NS, :]).then_inc(sc_done, 1)
            dve.wait_ge(sc_done, NPG // 4)
            with V.loop(0, 256 // 8, 2):
                take8(score[:, :], NS, top8b)
            V(ts(m16[:, :], score[:, :], TAKEN, NEG, ALU.not_equal, ALU.mult))
            phase(5)

            def attention(mx):
                N = 2 * H
                for h in range(H):
                    dve.wait_ge(strip_ps, mx * H + h + 1)
                    copy(strip[:, h, :], bank[h % 4][:, 0:384]).then_inc(strip_evac, 1)
                dve.wait_ge(strip_evac, mx * H + H)
                for n in range(N + 1):
                    if n < N:
                        t, h = n // H, n % H
                        nk = (t + 1) * P
                        off = P - t * P
                        dve.wait_ge(pl_done, mx * 2 * H + n + 1)
                        if n >= 2:
                            dve.wait_ge(pt_ps, mx * 2 * H + n - 1)
                        tt(lgP[:, n % 2, 0:nk], bank[n % 2][:, 0:nk], strip[:, h, off:off + nk], ALU.add)\
                            .then_inc(pl_evac, 1)
                        dve.wait_ge(pl_evac, mx * 2 * H + n + 1)
                        V(nc.vector.tensor_reduce(stP[:, n % 2, 0:1], lgP[:, n % 2, 0:nk], AX_X, ALU.max))
                        ts(stP[:, n % 2, 1:2], stP[:, n % 2, 0:1], -1.0, None, ALU.mult).then_inc(pm_done, 1)
                    if n >= 1:
                        m = n - 1
                        nk = (m // H + 1) * P
                        dve.wait_ge(px_done, mx * 2 * H + m + 1)
                        V(nc.vector.reciprocal(stP[:, m % 2, 3:4], stP[:, m % 2, 2:3]))
                        ts(lgP[:, m % 2, 0:nk], lgP[:, m % 2, 0:nk], stP[:, m % 2, 3:4], None, ALU.mult)\
                            .then_inc(pp_done, 1)
                dve.wait_ge(pp_done, mx * 2 * H + N)
                phase(6 + 3 * mx)

                def cur(b, s):
                    if mx == 0:
                        copy(ecur[:, s, :], eall[:, bass.ds(b, 1), :].rearrange("p o r -> p (o r)"))\
                            .then_inc(ecur_done, 1)

                def logits(b, s):
                    for c in range(4):
                        dve.wait_ge(lg_ps[mx], b * 5 + c + 1)
                        if mx == 1:
                            nc.vector.tensor_reduce(gate[:, 2 * c:2 * c + 2],
                                                    bank[c][0:NS, :].rearrange("p (o k) -> p o k", o=2), AX_X, ALU.add)\
                                .then_inc(gate_done, 1)
                    ts(lg[:, s, PAST - 512:PAST - P], bank[3][0:NS, 0:384], far[:, mx:mx + 1], None, ALU.add)
                    tt(lg[:, s, PAST - P:PAST], bank[3][0:NS, 384:512], near[:, mx, 0:P], ALU.add)
                    dve.wait_ge(lg_ps[mx], b * 5 + 5)
                    tt(lg[:, s, PAST:L], bank[6][0:NS, 0:TS], near[:, mx, P:P + TS], ALU.add)
                    V(copy(vnew[:, s, :], bank[6][0:TS, P:3 * P]))

                def maximum(b, s):
                    dve.wait_ge(lg_act[mx], b * 3 + 3)
                    if mx == 1:
                        dve.wait_ge(gate_done, b * 4 + 4)
                        V(nc.vector.memset(gate[:, 8:13], -TAKEN))
                        V(nc.vector.memset(gate[:, 13:16], NEG), wait_apart)
                        take8(gate[:, :], NS, top8b)
                        V(ts(gneg[:, :], gate[:, 0:8], TAKEN, NEG, ALU.not_equal, ALU.mult))
                        past = lg[:, s, 0:PAST].rearrange("p (o k) -> p o k", o=8)
                        V(tt(past, past, gneg[:, :].unsqueeze(2).to_broadcast([NS, 8, 256]), ALU.add))
                    V(nc.vector.tensor_reduce(stS[:, s, 0:1], lg[:, s, :], AX_X, ALU.max))
                    ts(stS[:, s, 1:2], stS[:, s, 0:1], -1.0, None, ALU.mult).then_inc(mx_done[mx], 1)

                def probs(b, s):
                    dve.wait_ge(ex_done[mx], b + 1)
                    V(nc.vector.reciprocal(stS[:, s, 3:4], stS[:, s, 2:3]))
                    ts(lg[:, s, :], lg[:, s, :], stS[:, s, 3:4], None, ALU.mult).then_inc(p_done[mx], 1)

                def output(b):
                    dve.wait_ge(pT_ps[mx], 2 * b + 2)
                    copy(pT[:, 8:16, :].rearrange("p k q -> p (k q)"), bank[5])
                    copy(pTn[:, :], bank[7][0:TS, NS:2 * NS]).then_inc(pT_dve[mx], 1)

                def step(b, s, more=True):
                    probs(b, s)
                    logits(b + 1, 1 - s)
                    output(b)
                    if more:
                        cur(b + 2, s)
                    maximum(b + 1, 1 - s)
                if mx == 0:
                    dve.wait_ge(eall_in, 16)
                dve.wait_ge(near_in, 16 * 2 * (TS + 1))
                cur(0, 0)
                cur(1, 1)
                logits(0, 0)
                maximum(0, 0)
                step(0, 0)
                with V.loop(0, NB // 2 - 2, 6 if mx == 0 else 18) as i:
                    step(2 * i + 1, 1)
                    step(2 * i + 2, 0)
                step(NB - 3, 1)
                step(NB - 2, 0, False)
                probs(NB - 1, 1)
                output(NB - 1)
                dve.wait_ge(pT_dve[mx], NB)
                phase(7 + 3 * mx, mx == 0)

            attention(0)
            dve_stage(dve, V, "B", nothing)
            phase(8)
            attention(1)

            def split_o(c):
                for g in O_GROUPS.get(c, ()):
                    dve.wait_ge(o_hi_done, g + 1)
                    gs = slice(4 * g, 4 * g + 4)
                    tt(o_lo[:, gs, :], o_stage[:, g % 2, :, :], o_hi[:, gs, :].bitcast(F32), ALU.subtract)\
                        .then_inc(o_split, 1)
            mj0 = STAGES["M"][3]

            def merge(j, i, q, used):
                if j % 2 == 0:
                    return
                dve.wait_ge(w_used, used)
                dve.wait_ge(bank_free[1 - q], (mj0 + j - 1) // 2 + 3 * i + 1)
                m2 = m_f[:, bass.ds(2 * i, 2), :]
                nth = (mj0 + j) // 2 + 3 * i + 1
                tt(m2 if j == 1 else term[:, :, :], sig[:, :, :], dense[:, 2 * q:2 * q + 2, 0:T], ALU.mult)\
                    .then_inc(bank_free[q], 1)
                dve.wait_ge(bank_free[q], nth)
                if j > 1:
                    V(tt(m2, m2, term[:, :, :], ALU.add))
            dve_stage(dve, V, "M", merge, 2, before=split_o)
            evacuated(dve, "M")
            phase(11)
            phase(12)
            dve.wait_ge(m_hi_done, 1)
            V(tt(m_lo[:, :, :], m_f[:, :, :], m_hi[:, :, :].bitcast(F32), ALU.subtract))
            phase(13)

            def into_x1(j, i, q, used):
                dve.wait_ge(w_used, used)
                x2 = x1[:, bass.ds(4 * i + 2 * j, 2), :]
                tt(x2, x2, dense[:, 2 * q:2 * q + 2, 0:T], ALU.add).then_inc(bank_free[q], 1)
            dve.wait_ge(x1_in, 16)
            dve_stage(dve, V, "O", into_x1)
            evacuated(dve, "O")
            phase(14)
            norm(x1, tmp1, gffn, 1, True)
            phase(15)
            dve.wait_ge(cw_in, 48)
            nc.vector.memset(ue[:, :, 0:2], 0.0).then_inc(ue_zero, 1)

            def ff(base, yb, nb):
                def evac(j, i, q, used):
                    n = base + i
                    if j == 0:
                        dve.wait_ge(ue_done, n + 1)
                        dve.wait_ge(g_done, n)
                        for b in range(nb):
                            f = 2 * n + b
                            src = (lambda k: ue[:, b, k:k + TP],
                                   lambda k: ue[:, b, 258:338].rearrange("p (r t) -> p r t", t=10)[:, :, k:k + TS])
                            dst = (cv[:, b, 0:TP], cv[:, b, TP:T].rearrange("p (r t) -> p r t", t=TS))

                            def w(k):
                                return cw[:, k, bass.ds(f, 1)]
                            for r in range(2):
                                ins = ts(dst[r], src[r](0), w(0), w(3), ALU.mult, ALU.add)
                            V(ins)
                            for k in (1, 2):
                                for r in range(2):
                                    ins = stt(dst[r], src[r](k), w(k), dst[r], ALU.mult, ALU.add)
                                if k == 1 or b < nb - 1:
                                    V(ins)
                        ins.then_inc(cv_made, 1)
                    else:
                        dve.wait_ge(w_used, used)
                        dve.wait_ge(g_done, n + 1)
                        nth = (STAGES["F1"][3] + 1) // 2
                        y2 = yv[:, 0:nb, :]
                        V(tt(y2, y2, dense[:, 2 * q:2 * q + nb, 0:T], ALU.mult))
                        dve.sem_inc(bank_free[q], 1)
                        dve.sem_inc(ym_done, 1)
                        dve.wait_ge(yh_done, n + 1)
                        yb2 = bass.ds(yb + 2 * i, nb)
                        tt(y_lo[:, yb2, :], y2, y_hi[:, yb2, :].bitcast(F32), ALU.subtract).then_inc(y_done, 1)
                return evac
            dve_stage(dve, V, "F1", ff(0, 0, 2), 6)
            dve.wait_ge(y_done, KF1 // 2)
            phase(16)
            dve_stage(dve, V, "D1", into_x1)
            dve_stage(dve, V, "F2", ff(KF1 // 2, 0, 2), 6)
            dve_stage(dve, V, "F3", ff(KF // 2, KF2 - 1, 1))
            dve.wait_ge(y_done, KF // 2 + 1)
            phase(17)
            dve_stage(dve, V, "D2", into_x1)
            evacuated(dve, "D2")
            phase(18)
            norm(x1, tmp1, gfin, 2, False)


def constants():
    f = np.float32
    c = {"c_ident": np.eye(P, dtype=f), "c_anti": np.eye(P, dtype=f)[::-1]}
    rot = np.zeros((P, P), f)
    for m in range(64):
        rot[m + 64, m] = -1
        rot[m, m + 64] = 1
    c["c_rot"] = rot
    pos = np.concatenate([np.arange(TP), np.tile(PAST + np.arange(TS), NB)]).astype(f)
    inv = f(10000.0) ** (-np.arange(0, DH, 2, dtype=f) / f(DH))
    ang = pos[None, :] * inv[:, None].astype(f)
    c["c_cos"] = np.concatenate([np.cos(ang)] * 2).astype(f)
    c["c_sin"] = np.concatenate([np.sin(ang)] * 2).astype(f)
    lg = np.log1p(-np.exp2(-5.0 - np.arange(H)))
    i = np.arange(P, dtype=np.float64)
    diff = i[None, :] - i[:, None]
    c["c_intrap"] = np.where(diff[:, None, :] >= 0, np.exp(np.maximum(diff, 0)[:, None, :] * lg[None, :, None]), 0).astype(f)
    r, q = np.arange(NS) // TS, np.arange(NS) % TS
    d8 = q[None, :] - q[:, None]
    ok = (r[None, :] == r[:, None]) & (d8 >= 0)
    c["c_intras"] = np.where(ok[:, None, :], np.exp(np.maximum(d8, 0)[:, None, :] * lg[None, :, None]), 0).astype(f)
    c["c_cross"] = np.broadcast_to(np.exp((i + 1)[None, :] * lg[:, None]), (P, H, P)).astype(f)
    c["c_tailp"] = np.exp((P - 1 - i)[:, None] * lg[None, :]).astype(f)
    c["c_tails"] = (np.exp((TS - 1 - q)[:, None, None] * lg[None, :, None])
                    * (r[:, None, None] == np.arange(NB)[None, None, :])).astype(f)
    c["c_decay"] = np.broadcast_to(np.exp(np.array([P, TS])[:, None] * lg[None, :]), (P, 2, H)).astype(f)
    dist = RD0 - np.arange(RVEC)
    n = np.maximum(dist, 0)
    half = NBUCK // 2
    nf = np.maximum(n, 1).astype(f)
    large = half + (np.log(nf / f(half)) / f(np.log(128 / half)) * f(NBUCK - half)).astype(np.int32)
    bucket = np.where(n < half, n, np.minimum(large, NBUCK - 1))
    one = np.zeros((NBUCK + 1, RVEC), f)
    one[np.where(dist < 0, NBUCK, bucket), np.arange(RVEC)] = 1
    c["c_onehot"] = one
    k = np.arange(TP)
    qpos = np.arange(P)[:, None] + P * np.arange(2)[None, :]
    c["c_causp"] = np.where(k[None, None, :] <= qpos[:, :, None], 0, NEG).astype(f)
    c["c_causs"] = np.where(np.arange(TS)[None, :] <= q[:, None], 0, NEG).astype(f)
    hq = np.arange(P) % TS
    c["c_sel"] = ((r[None, None, :] == np.arange(NB)[None, :, None]) & (q[None, None, :] == hq[:, None, None])).astype(f)
    c["c_eall"] = ((r[:, None, None] == np.arange(NB)[None, :, None]) & (q[:, None, None] == q[None, None, :])).astype(f)
    return {n: np.ascontiguousarray(v) for n, v in c.items()}


_INS = ['cache_a_v', 'cache_b_v', 'state_ret', 'page_table', 'rel_bias',
        'w_in', 'w_pa', 'w_pb', 'w_pc', 'w_out', 'ffn_up', 'ffn_gate', 'ffn_down']
_OUTS = [("y", (P, KD, T)), ("kv_a", (P, 4, T)), ("ki", (DI, T)), ("kv_b", (P, 4, T)),
         ("ret_p", (1, 1, H, DH, 256)), ("ret_s", (1, NB, H, DH, 256)), ("conv_end", (P, KF, 18))]


def lay_in(x):
    def features(v):
        v = np.asarray(v)
        return v.reshape(v.shape[0], -1, P).transpose(2, 1, 0)

    def blocks(v):
        return features(np.asarray(v).reshape(1, -1))[:, :, 0]

    def keys_last(v):
        v = np.asarray(v)
        return v.swapaxes(2, v.ndim - 1)

    return {
        "cache_a_k": keys_last(x["cache_a_k"]), "cache_b_k": keys_last(x["cache_b_k"]),
        "cache_a_kidx": keys_last(x["cache_a_kidx"]),
        "x": features(np.concatenate([np.asarray(x["x_prompt"])[0], np.asarray(x["x_sample"]).reshape(NS, D)])),
        "norm_mix": blocks(x["norm_mix"]), "norm_ffn": blocks(x["norm_ffn"]), "norm_final": blocks(x["norm_final"]),
        "ret_gn": blocks(x["ret_gn"]), "conv_b": blocks(x["conv_b"]),
        "conv_w": features(np.asarray(x["conv_w"])[0]).transpose(0, 2, 1),
        "state_conv": features(np.asarray(x["state_conv"]).reshape(2 * NB, DFF)),
    }


def lay_out(r):
    def rows(v):
        return v.transpose(2, 1, 0).reshape(v.shape[2], -1)

    y, end, ki = rows(r["y"]), rows(r["conv_end"]), r["ki"].T
    kv = []
    for m in "ab":
        v = rows(r["kv_" + m]).reshape(T, 2, HKV, DH)
        kv.append([v[:TP, 0][None, None], v[:TP, 1][None, None],
                   v[TP:, 0].reshape(1, NB, TS, HKV, DH), v[TP:, 1].reshape(1, NB, TS, HKV, DH)])
    (akp, avp, aks, avs), (bkp, bvp, bks, bvs) = kv
    return (y[:TP][None], y[TP:].reshape(NB, TS, D), akp, avp, ki[:TP][None, None], bkp, bvp, r["ret_p"],
            end[:2][None, None], aks, avs, ki[TP:].reshape(1, NB, TS, DI), bks, bvs, r["ret_s"],
            end[2:].reshape(1, NB, 2, DFF))


def kernel(**inputs):
    import concourse.bacc as _bacc
    from concourse.bass_utils import run_bass_kernel_spmd as _run

    nc = _bacc.Bacc("TRN2", target_bir_lowering=False, num_devices=1)
    arrays, a, out = {}, {}, {}
    for name, x in [(n, inputs[n]) for n in _INS] + sorted(lay_in(inputs).items()) + sorted(constants().items()):
        x = np.ascontiguousarray(x)
        arrays[f"in_{name}"] = x
        a[name] = nc.dram_tensor(f"in_{name}", x.shape, mybir.dt.from_np(x.dtype), kind="ExternalInput").ap()
    for name, shape in _OUTS:
        out[name] = nc.dram_tensor(f"out_{name}", shape, F32, kind="ExternalOutput").ap()
    build(nc, a, out)
    r = _run(nc, [arrays], core_ids=[0])
    return tuple(np.ascontiguousarray(v) for v in lay_out({n: r.results[0][f"out_{n}"] for n, _ in _OUTS}))
```
